# Optimizing a Trainium2 kernel written in Bass

```python
import math
import jax, jax.numpy as jnp
from jax import lax
import numpy as np

D_MODEL = 1024
BATCH = 1
SEQ = 512
DEPTH = 1
DEC_BATCH = 1
DEC_SEQ = 64
PAST_LEN = 512

CHUNK = 64
SSM_WIDTH = D_MODEL
SSM_GROUP = 16
SSM_GROUPS = SSM_WIDTH // SSM_GROUP
SSM_STATE = 64
N_HEADS = 16
HEAD_DIM = 64
N_KV_HEADS = 4
Q_PER_KV = N_HEADS // N_KV_HEADS
ATT_WIDTH = N_HEADS * HEAD_DIM
KV_WIDTH = N_KV_HEADS * HEAD_DIM
WINDOW = 128
WIN_CHUNKS = WINDOW // CHUNK
N_MEM = 256
X_HEADS = 4
X_HEAD_DIM = D_MODEL // X_HEADS
X_WIDTH = X_HEADS * X_HEAD_DIM
D_FF = 4 * D_MODEL
EPS = 1e-6
NEG_INF = -1e30
OFF_Q = SSM_WIDTH
OFF_K = OFF_Q + ATT_WIDTH
OFF_V = OFF_K + KV_WIDTH
OFF_GS = OFF_V + KV_WIDTH
OFF_GA = OFF_GS + D_MODEL
IN_WIDTH = OFF_GA + D_MODEL

kernel_name = "hybrid_s5_swa_streaming_step"

def rmsnorm(x, g):
    x32 = x.astype(jnp.float32)
    y = x32 * lax.rsqrt(jnp.mean(x32 * x32, axis=-1, keepdims=True) + EPS) * g.astype(jnp.float32)
    return y.astype(x.dtype)

def cmul(ar, ai, br, bi):
    return ar * br - ai * bi, ar * bi + ai * br

def alibi_slopes():
    h = jnp.arange(1, N_HEADS + 1, dtype=jnp.float32)
    return jnp.exp2(-8.0 * h / N_HEADS)

def ssm_discretize(a_re, a_im, log_dt, b_re, b_im):
    dt = jnp.exp(log_dt.astype(jnp.float32))[:, None]
    ar = a_re.astype(jnp.float32)
    ai = a_im.astype(jnp.float32)
    mag = jnp.exp(dt * ar)
    abar_re = mag * jnp.cos(dt * ai)
    abar_im = mag * jnp.sin(dt * ai)
    den = ar * ar + ai * ai
    nr = abar_re - 1.0
    ni = abar_im
    f_re = (nr * ar + ni * ai) / den
    f_im = (ni * ar - nr * ai) / den
    br = b_re.astype(jnp.float32)
    bi = b_im.astype(jnp.float32)
    bbar_re, bbar_im = cmul(f_re[..., None], f_im[..., None], br, bi)
    return abar_re, abar_im, bbar_re, bbar_im

def scan_combine(e1, e2):
    a1r, a1i, b1r, b1i = e1
    a2r, a2i, b2r, b2i = e2
    ar, ai = cmul(a2r, a2i, a1r, a1i)
    br, bi = cmul(a2r, a2i, b1r, b1i)
    return ar, ai, br + b2r, bi + b2i

def ssm_block(u, h_re, h_im, disc, c_re, c_im):
    abar_re, abar_im, bbar_re, bbar_im = disc
    bsz, length = u.shape[0], u.shape[1]
    ug = u.reshape(bsz, length, SSM_GROUPS, SSM_GROUP)
    bu_re = jnp.einsum('blgk,gpk->blgp', ug, bbar_re)
    bu_im = jnp.einsum('blgk,gpk->blgp', ug, bbar_im)
    ah_re, ah_im = cmul(abar_re, abar_im, h_re, h_im)
    bu_re = bu_re.at[:, 0].add(ah_re)
    bu_im = bu_im.at[:, 0].add(ah_im)
    a_re = jnp.broadcast_to(abar_re, bu_re.shape)
    a_im = jnp.broadcast_to(abar_im, bu_im.shape)
    _, _, s_re, s_im = lax.associative_scan(scan_combine, (a_re, a_im, bu_re, bu_im), axis=1)
    y = (jnp.einsum('blgp,gkp->blgk', s_re, c_re.astype(jnp.float32))
         - jnp.einsum('blgp,gkp->blgk', s_im, c_im.astype(jnp.float32)))
    return y.reshape(bsz, length, SSM_WIDTH), s_re[:, -1], s_im[:, -1]

def ssm_prompt(u, disc, c_re, c_im):
    bsz, length = u.shape[0], u.shape[1]
    n_chunks = length // CHUNK
    ub = u.reshape(bsz, n_chunks, CHUNK, SSM_WIDTH).transpose(1, 0, 2, 3)
    h0 = jnp.zeros((bsz, SSM_GROUPS, SSM_STATE), jnp.float32)

    def step(carry, u_blk):
        y_blk, hr, hi = ssm_block(u_blk, carry[0], carry[1], disc, c_re, c_im)
        return (hr, hi), y_blk

    (h_re, h_im), y = lax.scan(step, (h0, h0), ub)
    return y.transpose(1, 0, 2, 3).reshape(bsz, length, SSM_WIDTH), h_re, h_im

def band_attention(q, k, v, key_valid, sinks):
    nq, ns = q.shape[2], k.shape[2]
    scores = jnp.einsum('bnqkrd,bnskd->bnkrqs', q, k).astype(jnp.float32) * (HEAD_DIM ** -0.5)
    dist = jnp.abs(WINDOW + jnp.arange(nq)[:, None] - jnp.arange(ns)[None, :]).astype(jnp.float32)
    slopes = alibi_slopes().reshape(N_KV_HEADS, Q_PER_KV)[:, :, None, None]
    scores = scores - slopes * dist
    scores = jnp.where(key_valid[None, :, None, None, None, :], scores, NEG_INF)
    sink = sinks.astype(jnp.float32).reshape(N_KV_HEADS, Q_PER_KV)[:, :, None, None]
    m = jnp.maximum(jnp.max(scores, axis=-1, keepdims=True), sink)
    p = jnp.exp(scores - m)
    denom = jnp.sum(p, axis=-1, keepdims=True) + jnp.exp(sink - m)
    probs = (p / denom).astype(v.dtype)
    return jnp.einsum('bnkrqs,bnskd->bnqkrd', probs, v)

def swa_prompt(q, k, v, sinks):
    bsz, length = q.shape[0], q.shape[1]
    n_chunks = length // CHUNK
    qb = q.reshape(bsz, n_chunks, CHUNK, N_KV_HEADS, Q_PER_KV, HEAD_DIM)

    def band(t):
        tp = jnp.pad(t, ((0, 0), (WINDOW, 0), (0, 0), (0, 0)))
        blocks = tp.reshape(bsz, n_chunks + WIN_CHUNKS, CHUNK, N_KV_HEADS, HEAD_DIM)
        return jnp.concatenate([blocks[:, w:w + n_chunks] for w in range(WIN_CHUNKS + 1)], axis=2)

    key_pos = jnp.arange(n_chunks)[:, None] * CHUNK - WINDOW + jnp.arange(WINDOW + CHUNK)[None, :]
    out = band_attention(qb, band(k), band(v), key_pos >= 0, sinks)
    return out.reshape(bsz, length, ATT_WIDTH), k[:, -WINDOW:], v[:, -WINDOW:]

def swa_sample(q, k, v, cache_k, cache_v, sinks):
    bsz, nq = q.shape[0], q.shape[1]
    kk = jnp.concatenate([cache_k, k], axis=1)
    vv = jnp.concatenate([cache_v, v], axis=1)
    qb = q.reshape(bsz, 1, nq, N_KV_HEADS, Q_PER_KV, HEAD_DIM)
    valid = jnp.ones((1, WINDOW + nq), dtype=bool)
    out = band_attention(qb, kk[:, None], vv[:, None], valid, sinks)
    return out.reshape(bsz, nq, ATT_WIDTH), kk[:, -WINDOW:], vv[:, -WINDOW:]

def cross_attention(h, mk, mv, w_xq, w_xo):
    bsz, length = h.shape[0], h.shape[1]
    q = (h @ w_xq).reshape(bsz, length, X_HEADS, X_HEAD_DIM)
    s = jnp.einsum('blhd,bmhd->bhlm', q, mk).astype(jnp.float32) * (X_HEAD_DIM ** -0.5)
    p = jax.nn.softmax(s, axis=-1).astype(mv.dtype)
    o = jnp.einsum('bhlm,bmhd->blhd', p, mv).reshape(bsz, length, X_WIDTH)
    return o @ w_xo

def layer_forward(x, lp, mem_kv, ssm_h, win_kv):
    bsz, length = x.shape[0], x.shape[1]
    h = rmsnorm(x, lp['norm_mix_pre'])
    z = h @ lp['w_in']
    u, q, k, v, g_s, g_a = jnp.split(z, [OFF_Q, OFF_K, OFF_V, OFF_GS, OFF_GA], axis=-1)
    q = q.reshape(bsz, length, N_HEADS, HEAD_DIM)
    k = k.reshape(bsz, length, N_KV_HEADS, HEAD_DIM)
    v = v.reshape(bsz, length, N_KV_HEADS, HEAD_DIM)
    disc = ssm_discretize(lp['ssm_a_re'], lp['ssm_a_im'], lp['ssm_log_dt'], lp['ssm_b_re'], lp['ssm_b_im'])
    u32 = u.astype(jnp.float32)
    if ssm_h is None:
        y_ssm, h_re, h_im = ssm_prompt(u32, disc, lp['ssm_c_re'], lp['ssm_c_im'])
        att, win_k, win_v = swa_prompt(q, k, v, lp['attn_sinks'])
    else:
        y_ssm, h_re, h_im = ssm_block(u32, ssm_h[0], ssm_h[1], disc, lp['ssm_c_re'], lp['ssm_c_im'])
        att, win_k, win_v = swa_sample(q, k, v, win_kv[0], win_kv[1], lp['attn_sinks'])
    y_ssm = jax.nn.gelu(y_ssm + lp['ssm_d'].astype(jnp.float32) * u32)
    y_ssm = (y_ssm * jax.nn.sigmoid(y_ssm @ lp['w_glu'])).astype(x.dtype)
    mixed = jax.nn.sigmoid(g_s) * (y_ssm @ lp['p_ssm']) + jax.nn.sigmoid(g_a) * (att @ lp['p_att'])
    x = x + rmsnorm(mixed @ lp['w_out'], lp['norm_mix_post'])
    h = rmsnorm(x, lp['norm_x_pre'])
    x = x + rmsnorm(cross_attention(h, mem_kv[0], mem_kv[1], lp['w_xq'], lp['w_xo']), lp['norm_x_post'])
    h = rmsnorm(x, lp['norm_ff_pre'])
    x = x + rmsnorm(jnp.square(jax.nn.relu(h @ lp['w_ff1'])) @ lp['w_ff2'], lp['norm_ff_post'])
    return x, (win_k, win_v, h_re, h_im)

def setup_inputs(seed: int = 0) -> dict:
    key = jax.random.key(seed)
    ks = iter(jax.random.split(key, 48))
    f32 = jnp.float32

    def nrm(shape, scale):
        return jax.random.normal(next(ks), shape, f32) * scale

    def gain():
        return 1.0 + nrm((DEPTH, D_MODEL), 0.05)

    a_im = jnp.pi * jnp.arange(SSM_STATE, dtype=f32)
    return {
        'x_prompt': nrm((BATCH, SEQ, D_MODEL), 1.0),
        'x_sample': nrm((DEC_BATCH, DEC_SEQ, D_MODEL), 1.0),
        'mem_prompt': nrm((BATCH, N_MEM, D_MODEL), 1.0),
        'cache_win_k': nrm((DEPTH, DEC_BATCH, WINDOW, N_KV_HEADS, HEAD_DIM), 1.0),
        'cache_win_v': nrm((DEPTH, DEC_BATCH, WINDOW, N_KV_HEADS, HEAD_DIM), 1.0),
        'state_ssm_re': nrm((DEPTH, DEC_BATCH, SSM_GROUPS, SSM_STATE), 0.3),
        'state_ssm_im': nrm((DEPTH, DEC_BATCH, SSM_GROUPS, SSM_STATE), 0.3),
        'cache_mem_k': nrm((DEPTH, DEC_BATCH, N_MEM, X_HEADS, X_HEAD_DIM), 1.0),
        'cache_mem_v': nrm((DEPTH, DEC_BATCH, N_MEM, X_HEADS, X_HEAD_DIM), 1.0),
        'norm_mix_pre': gain(),
        'norm_mix_post': gain(),
        'w_in': nrm((DEPTH, D_MODEL, IN_WIDTH), D_MODEL ** -0.5),
        'ssm_a_re': -0.5 + nrm((DEPTH, SSM_GROUPS, SSM_STATE), 0.01),
        'ssm_a_im': a_im + nrm((DEPTH, SSM_GROUPS, SSM_STATE), 0.01),
        'ssm_log_dt': jax.random.uniform(next(ks), (DEPTH, SSM_GROUPS), f32, math.log(1e-3), math.log(1e-1)),
        'ssm_b_re': nrm((DEPTH, SSM_GROUPS, SSM_STATE, SSM_GROUP), (2 * SSM_GROUP) ** -0.5),
        'ssm_b_im': nrm((DEPTH, SSM_GROUPS, SSM_STATE, SSM_GROUP), (2 * SSM_GROUP) ** -0.5),
        'ssm_c_re': nrm((DEPTH, SSM_GROUPS, SSM_GROUP, SSM_STATE), SSM_STATE ** -0.5),
        'ssm_c_im': nrm((DEPTH, SSM_GROUPS, SSM_GROUP, SSM_STATE), SSM_STATE ** -0.5),
        'ssm_d': nrm((DEPTH, SSM_WIDTH), 1.0),
        'w_glu': nrm((DEPTH, SSM_WIDTH, SSM_WIDTH), SSM_WIDTH ** -0.5),
        'attn_sinks': nrm((DEPTH, N_HEADS), 0.5),
        'p_ssm': nrm((DEPTH, SSM_WIDTH, D_MODEL), SSM_WIDTH ** -0.5),
        'p_att': nrm((DEPTH, ATT_WIDTH, D_MODEL), ATT_WIDTH ** -0.5),
        'w_out': nrm((DEPTH, D_MODEL, D_MODEL), D_MODEL ** -0.5),
        'norm_x_pre': gain(),
        'norm_x_post': gain(),
        'norm_mem': gain(),
        'w_xq': nrm((DEPTH, D_MODEL, X_WIDTH), D_MODEL ** -0.5),
        'w_xk': nrm((DEPTH, D_MODEL, X_WIDTH), D_MODEL ** -0.5),
        'w_xv': nrm((DEPTH, D_MODEL, X_WIDTH), D_MODEL ** -0.5),
        'w_xo': nrm((DEPTH, X_WIDTH, D_MODEL), X_WIDTH ** -0.5),
        'norm_ff_pre': gain(),
        'norm_ff_post': gain(),
        'w_ff1': nrm((DEPTH, D_MODEL, D_FF), D_MODEL ** -0.5),
        'w_ff2': nrm((DEPTH, D_FF, D_MODEL), D_FF ** -0.5),
    }

def reference(x_prompt, x_sample, mem_prompt, cache_win_k, cache_win_v, state_ssm_re, state_ssm_im,
              cache_mem_k, cache_mem_v, norm_mix_pre, norm_mix_post, w_in, ssm_a_re, ssm_a_im, ssm_log_dt,
              ssm_b_re, ssm_b_im, ssm_c_re, ssm_c_im, ssm_d, w_glu, attn_sinks, p_ssm, p_att, w_out,
              norm_x_pre, norm_x_post, norm_mem, w_xq, w_xk, w_xv, w_xo, norm_ff_pre, norm_ff_post,
              w_ff1, w_ff2):
    params = dict(norm_mix_pre=norm_mix_pre, norm_mix_post=norm_mix_post, w_in=w_in,
                  ssm_a_re=ssm_a_re, ssm_a_im=ssm_a_im, ssm_log_dt=ssm_log_dt, ssm_b_re=ssm_b_re,
                  ssm_b_im=ssm_b_im, ssm_c_re=ssm_c_re, ssm_c_im=ssm_c_im, ssm_d=ssm_d, w_glu=w_glu,
                  attn_sinks=attn_sinks, p_ssm=p_ssm, p_att=p_att, w_out=w_out,
                  norm_x_pre=norm_x_pre, norm_x_post=norm_x_post, norm_mem=norm_mem,
                  w_xq=w_xq, w_xk=w_xk, w_xv=w_xv, w_xo=w_xo,
                  norm_ff_pre=norm_ff_pre, norm_ff_post=norm_ff_post, w_ff1=w_ff1, w_ff2=w_ff2)
    bp = mem_prompt.shape[0]
    xp, xs = x_prompt, x_sample
    wkp, wvp, srp, sip, mkp, mvp = [], [], [], [], [], []
    wks, wvs, srs, sis = [], [], [], []
    for l in range(DEPTH):
        lp = {name: arr[l] for name, arr in params.items()}
        mm = rmsnorm(mem_prompt, lp['norm_mem'])
        mk = (mm @ lp['w_xk']).reshape(bp, N_MEM, X_HEADS, X_HEAD_DIM)
        mv = (mm @ lp['w_xv']).reshape(bp, N_MEM, X_HEADS, X_HEAD_DIM)
        xp, (k_p, v_p, hr_p, hi_p) = layer_forward(xp, lp, (mk, mv), None, None)
        ssm_h = (state_ssm_re[l].astype(jnp.float32), state_ssm_im[l].astype(jnp.float32))
        xs, (k_s, v_s, hr_s, hi_s) = layer_forward(xs, lp, (cache_mem_k[l], cache_mem_v[l]), ssm_h,
                                                  (cache_win_k[l], cache_win_v[l]))
        wkp.append(k_p); wvp.append(v_p); srp.append(hr_p); sip.append(hi_p)
        mkp.append(mk); mvp.append(mv)
        wks.append(k_s); wvs.append(v_s); srs.append(hr_s); sis.append(hi_s)
    y_prompt, y_sample = xp, xs
    win_k_prompt = jnp.stack(wkp)
    win_v_prompt = jnp.stack(wvp)
    ssm_re_prompt = jnp.stack(srp)
    ssm_im_prompt = jnp.stack(sip)
    mem_k_prompt = jnp.stack(mkp)
    mem_v_prompt = jnp.stack(mvp)
    win_k_sample = jnp.stack(wks)
    win_v_sample = jnp.stack(wvs)
    ssm_re_sample = jnp.stack(srs)
    ssm_im_sample = jnp.stack(sis)
    return (y_prompt, y_sample, win_k_prompt, win_v_prompt, ssm_re_prompt, ssm_im_prompt,
            mem_k_prompt, mem_v_prompt, win_k_sample, win_v_sample, ssm_re_sample, ssm_im_sample)


_drawn_inputs = setup_inputs


def setup_inputs(seed=0):
    import zlib

    import numpy as np

    out = dict(_drawn_inputs(seed))
    spreads = {}
    factors = {'ssm_a_re': 54.385, 'attn_sinks': 6.217}
    for name, (base, spread) in spreads.items():
        noise = np.random.default_rng([zlib.crc32(name.encode()), seed]).standard_normal(out[name].shape)
        drawn = base * np.exp(spread * noise) if base else spread * noise
        out[name] = __import__('jax').numpy.asarray(drawn.astype(out[name].dtype))
    for name, factor in factors.items():
        out[name] = (out[name] * factor).astype(out[name].dtype)
    return out
```

```python
import math
from contextlib import ExitStack

import concourse.bass as bass
from concourse import mybir

F32 = mybir.dt.float32
F32R = mybir.dt.float32r
I32 = mybir.dt.int32
ACT = mybir.ActivationFunctionType
ALU = mybir.AluOpType
AX = mybir.AxisListType

P = 128
D = 1024
KT = D // P
TP, TS = 512, 64
TT = TP + TS
HT = TT // 2
EPS = 1e-6
NMEM = 256
CH = 64
NKV, HD = 4, 64
KV = NKV * HD
PAIRS = 32
SB = 4
NB = TT // SB
NBP = TP // SB
PB = 4
MAGIC = 1.5 * 2.0 ** 23
TWO_PI = 2 * math.pi
C1 = 6.28125
C2 = 0.0019350051879882812
C3 = TWO_PI - C1 - C2

T_Z, T_PATT, T_GLU, T_PSSM, T_WOUT = 0, 36, 44, 52, 60
T_XK, T_XV, T_XQ, T_XO, T_FF = 68, 76, 84, 92, 100
QUARTERS = 4
T_END = T_FF + 16 * QUARTERS
AHEAD = 3
SSM_SLABS = {m: list(range(12 + 4 * m, 16 + 4 * m)) for m in range(-1, 5)}
SSM_SLABS[5], SSM_SLABS[6] = [32, 33], [34, 35]

G_MIX_PRE, G_MIX_POST, G_X_PRE, G_X_POST, G_MEM, G_FF_PRE, G_FF_POST, G_D = range(8)
VEC_ROWS = ("norm_mix_pre", "norm_mix_post", "norm_x_pre", "norm_x_post", "norm_mem", "norm_ff_pre", "norm_ff_post",
            "ssm_d")


class Chain:

    def __init__(self, eng, sem):
        self.eng, self.sem, self.base, self.k, self.i, self.per = eng, sem, 0, 0, None, 0

    def __call__(self, ins):
        self.k += 1
        ins.then_inc(self.sem, 1)
        self.eng.wait_ge(self.sem, self.base + self.k + (0 if self.i is None else self.i * self.per))

    def enter(self, i, first, per):
        self.base += self.k - first * per
        self.k, self.i, self.per, self.first = 0, i, per, first

    def leave(self, end):
        assert self.k == self.per, (self.k, self.per)
        self.base += end * self.per
        self.k, self.i = 0, None


def build(nc, a):
    ds = bass.ds
    ctx = ExitStack()
    with ctx:
        def at(off, name, shape, dt=F32):
            with ExitStack() as s:
                if off:
                    s.enter_context(nc.sbuf_tensor(f"below_{name}", [P, off // 4], F32))
                return s.enter_context(nc.sbuf_tensor(name, shape, dt))

        X0 = 5120
        A0 = X0 + KT * TT * 4
        W0 = A0 + 2 * KT * TT * 4
        N0 = W0 + 10 * KT * P * 4
        Z0 = N0 + 5 * TT * 4
        S0 = Z0 + 20 * TT * 4
        ident = at(0, "ident", [P, P])
        ones = at(512, "ones", [P, P])
        gains = at(1024, "gains", [P, 64])
        eps = at(1280, "eps", [P, 1])
        halfpi = at(1312, "halfpi", [P, 1])
        sink = at(1344, "sink", [P, 8])
        cidx = at(1376, "cidx", [P, NB])
        cmask = at(1952, "cmask", [P, NB])
        fin = at(2528, "fin", [P, 2, PAIRS, 2])
        init = at(3040, "init", [P, 2, PAIRS])
        a4init = at(3296, "a4init", [P, 2, PAIRS])
        mstat = at(3552, "mstat", [P, 8])
        negm = at(3584, "negm", [P, 2, 8])
        den = at(3648, "den", [P, 2, 8])
        rden = at(3712, "rden", [P, 2, 8])
        esink = at(3776, "esink", [P, 2, 8])
        memss = at(3840, "memss", [P, 8])
        mxw = at(3872, "mxw", [P, 8])
        xss = at(3904, "xss", [P, 3, 8])
        x = at(X0, "x", [P, KT, TT])
        aH = at(A0, "aH", [P, KT, TT], F32R)
        aL = at(A0 + KT * TT * 4, "aL", [P, KT, TT], F32R)
        wraw = [at(W0 + s * 4096, f"wraw{s}", [P, KT, P]) for s in range(2)]
        wH = [at(W0 + (2 + s) * 4096, f"wH{s}", [P, KT, P], F32R) for s in range(4)]
        wL = [at(W0 + (6 + s) * 4096, f"wL{s}", [P, KT, P], F32R) for s in range(4)]
        sq = at(N0, "sq", [P, 2, TT])
        raw = at(N0 + 2 * TT * 4, "raw", [P, 2, TT])
        rstd = at(N0 + 4 * TT * 4, "rstd", [P, TT])
        z = at(Z0, "z", [P, 20, TT])
        Q0 = Z0 + 8 * TT * 4
        K0 = Z0 + 16 * TT * 4
        xin = at(Q0, "xin", [P, 5, D])
        xn = at(Z0, "xn", [P, 2, D])
        xsq = [at(X0 + i * 4096, f"xsq{i}", [P, D]) for i in range(4)] + [at(N0, "xsq4", [P, D])]
        craw = at(Q0 + 20480, "craw", [P, 2, 8, HD])
        st5 = at(Q0 + 24576, "st5", [PAIRS, 5, P])
        vecs = at(Q0 + 27136, "vecs", [64, P])
        off = [S0]

        def nxt(name, shape, dt=F32):
            n = 4
            for s in shape[1:]:
                n *= s
            r = at(off[0], name, shape, dt)
            off[0] += (n + 31) // 32 * 32
            return r

        btab = nxt("btab", [P, 2, 16, PAIRS])
        ctab = nxt("ctab", [P, 2, PAIRS, 16])
        pw = nxt("pw", [P, 2, 5, PAIRS])
        xm = nxt("xm", [P, 2, PB, SB, 32])
        zm = [nxt("zm0", [P, 2, PB, SB + 1, 32])]
        dz = at(off[0], "dz", [P, 32, PAIRS])
        xt = nxt("xt", [P, 2, PB, P])
        toep = [nxt("toep0", [P, PB, P])]
        rho = [nxt("rho0", [P, PB, NB])]
        prod = nxt("prod", [P, 2, PB, SB + 1, 16])
        braw = at(off[0], "braw", [PAIRS, 2, P, 16])
        rot = nxt("rot", [P, 4, PB, NB])
        hs = nxt("hs", [P, 2, PB, NB + 1])
        ub, er, ei = ([nxt(f"{n}0", [P, PB, NB])] for n in ("ub", "er", "ei"))
        assert off[0] <= S0 + 52700, off[0] - S0
        off[0] = X0
        zm.append(nxt("zm1", [P, 2, PB, SB + 1, 32]))
        toep.append(nxt("toep1", [P, PB, P]))
        for n, l in (("rho", rho), ("ub", ub), ("er", er), ("ei", ei)):
            l.append(nxt(f"{n}1", [P, PB, NB]))
        assert off[0] <= A0
        fb = at(N0 + 4 * TT * 4, "fb", [P, 2, SB, PAIRS])
        npwi = at(N0 + 4 * TT * 4 + 1024, "npwi", [P, 5, PAIRS])
        thl = at(N0 + 4 * TT * 4 + 1664, "thl", [P, 3, PAIRS])
        earg = raw
        sc = [at(A0 + b * 6144, f"sc{b}", [P, 8, 192]) for b in range(2)]
        qc = [at(A0 + 28672 + b * 4096, f"qc{b}", [P, 8, 2, CH]) for b in range(2)]
        off[0] = A0 + 12288
        vp = nxt("vp", [P, 9, KV])
        bias = nxt("bias", [P, 8, 192])
        dist = nxt("dist", [P, 192])
        assert off[0] <= A0 + 28672
        disti = at(A0 + 6144, "disti", [P, 192], I32)
        off[0] = S0
        cv = nxt("cv", [P, KV])
        ck = nxt("ck", [P, KV])
        ks = nxt("ks", [P, 2, 192])
        osb = [nxt(f"osb{b}", [P, 8, HD]) for b in range(2)]
        kout = nxt("kout", [P, 2, KV])
        fout = nxt("fout", [PAIRS, 4, P])
        pta = [nxt(f"pta{b}", [P, 8, P]) for b in range(2)]
        ptb = [nxt(f"ptb{b}", [64, 8, P]) for b in range(2)]
        cidi = at(S0, "cidi", [P, NB], I32)
        m1 = at(Q0, "m1", [P, KT, TT])
        bH = at(S0, "bH", [P, KT, TT], F32R)
        bL = at(S0 + KT * TT * 4, "bL", [P, KT, TT], F32R)
        gate = at(S0 + 36864, "gate", [P, 2, TT])
        gsig = at(S0 + 36864 + 2 * TT * 4, "gsig", [P, 2, TT])
        o = at(Z0, "o", [P, KT, TT])
        mmH = at(K0, "mmH", [P, KT, NMEM], F32R)
        mmL = at(S0 + 36864, "mmL", [P, KT, NMEM], F32R)
        memr = at(S0 + 45056, "memr", [P, D])
        memn = at(N0 + 2 * TT * 4, "memn", [P, D])
        mk = at(S0, "mk", [P, 2, D])
        mv = at(S0 + 8192, "mv", [P, 2, D])
        mkT = at(S0 + 16384, "mkT", [P, KT, NMEM])
        smk = at(S0 + 24576, "smk", [P, 2, D])
        mvT = at(S0 + 32768, "mvT", [P, 2, NMEM])
        smkT = at(Q0, "smkT", [P, KT, NMEM])
        smv = at(Q0 + 8192, "smv", [P, 2, D])
        xq = at(Z0, "xq", [P, KT, TT])
        pc = [at(S0 + 32768 + b * 4096, f"pc{b}", [P, 4, NMEM]) for b in range(2)]
        ptc = at(S0 + 40960, "ptc", [P, 4, 2, P])
        yst = at(S0, "yst", [P, 5, D])

        gp = ctx.enter_context(nc.psum_tensor("gp", [P, 4, 512], F32))
        sp_ = ctx.enter_context(nc.psum_tensor("sp", [P, 4, 512], F32))
        x_copy = nc.dram_tensor("x_scratch", (P, KT * TT), F32).ap()
        gates = nc.dram_tensor("gates_scratch", (16, P, TT), F32).ap()

        def sem(name):
            return ctx.enter_context(nc.semaphore(name))

        x_loaded = [sem(f"x_loaded{i}") for i in range(5)]
        x_spilled = sem("x_spilled")
        x_back = sem("x_back")
        v_read = sem("v_read")
        vecs_loaded = sem("vecs_loaded")
        st5_loaded = sem("st5_loaded")
        c_loaded = sem("c_loaded")
        b_loaded = sem("b_loaded")
        w_loaded = [sem(f"w_loaded{s}") for s in range(2)]
        gate_stored = [sem(f"gate_stored{s}") for s in range(2)]
        gate_loaded = [sem(f"gate_loaded{s}") for s in range(2)]
        cache_loaded = sem("cache_loaded")
        sink_loaded = sem("sink_loaded")
        mem_loaded = [sem(f"mem_loaded{s}") for s in range(2)]
        smk_loaded = sem("smk_loaded")
        smv_loaded = sem("smv_loaded")
        stored = sem("stored")
        state_stored = sem("state_stored")
        mem_stored = sem("mem_stored")
        wh_done = sem("wh_done")
        wl_done = sem("wl_done")
        gemm_done = sem("gemm_done")
        evac_act = sem("evac_act")
        evac_dve = sem("evac_dve")
        in_h = sem("in_h")
        in_l = sem("in_l")
        raw_ready = sem("raw_ready")
        const_ready = sem("const_ready")
        ones_ready = sem("ones_ready")
        dt_ready = sem("dt_ready")
        xr_ready = sem("xr_ready")
        xnt_ready = sem("xnt_ready")
        xnt_ps = sem("xnt_ps")
        xh_done = sem("xh_done")
        xl_done = sem("xl_done")
        xt_ps = sem("xt_ps")
        xt_cp = sem("xt_cp")
        g_ps = sem("g_ps")
        g_cp = sem("g_cp")
        sq_ready = sem("sq_ready")
        sq_used = sem("sq_used")
        root_ready = sem("root_ready")
        st_ps = sem("st_ps")
        st_cp = sem("st_cp")
        disc_v = sem("disc_v")
        disc_a = sem("disc_a")
        coef_ready = sem("coef_ready")
        tab_ready = sem("tab_ready")
        x_tab = sem("x_tab")
        tab_ps = sem("tab_ps")
        xtab_cp = sem("xtab_cp")
        toep_cp = sem("toep_cp")
        earg_ready = sem("earg_ready")
        trig_ready = sem("trig_ready")
        e_ready = sem("e_ready")
        u_built = sem("u_built")
        v_ps = sem("v_ps")
        h_ready = sem("h_ready")
        y_ps = sem("y_ps")
        y_evac = sem("y_evac")
        gelu_done = sem("gelu_done")
        fin_ps = sem("fin_ps")
        fin_cp = sem("fin_cp")
        va_ps = sem("va_ps")
        va_cp = sem("va_cp")
        bias_ready = sem("bias_ready")
        dist_ready = sem("dist_ready")
        qzero = sem("qzero")
        qc_ready = sem("qc_ready")
        s_ps = sem("s_ps")
        s_read = sem("s_read")
        m_ready = sem("m_ready")
        p_ready = sem("p_ready")
        es_ready = sem("es_ready")
        pt_ps = sem("pt_ps")
        pta_cp = sem("pta_cp")
        ptb_cp = sem("ptb_cp")
        o_ps = sem("o_ps")
        o_cp = sem("o_cp")
        ot_ps = sem("ot_ps")
        att_done = sem("att_done")
        gsig_ready = sem("gsig_ready")
        mn_ready = sem("mn_ready")
        mm_ps = sem("mm_ps")
        mmh_done = sem("mmh_done")
        mml_done = sem("mml_done")
        memr_used = sem("memr_used")
        kvt_ps = sem("kvt_ps")
        kvt_cp = sem("kvt_cp")
        smk_ps = sem("smk_ps")
        smk_cp = sem("smk_cp")
        xs_ps = sem("xs_ps")
        xs_read = sem("xs_read")
        xm_ready = sem("xm_ready")
        xp_ready = sem("xp_ready")
        xn_ready = sem("xn_ready")
        xpt_ps = sem("xpt_ps")
        xpt_cp = sem("xpt_cp")
        xo_ps = sem("xo_ps")
        ca_h = sem("ca_h")
        ca_l = sem("ca_l")
        x_done = sem("x_done")
        yt_ps = sem("yt_ps")
        yt_cp = sem("yt_cp")
        act_seq = sem("act_seq")
        dve_seq = sem("dve_seq")
        pool_seq = sem("pool_seq")

        w_of = {n: a[n][0].rearrange("(k p) c -> p k c", p=P)
                for n in ("w_in", "p_att", "w_glu", "p_ssm", "w_out", "w_xk", "w_xv", "w_xq", "w_xo", "w_ff1")}
        w_ff2 = a["w_ff2"][0].rearrange("(k p) c -> p k c", p=P)
        tok = [(i * P, min(P, TT - i * P)) for i in range(5)]

        IN_X0, IN_ATT, IN_Y, IN_Y2, IN_MIX, IN_X1, IN_X2, IN_FF = (8 * n for n in range(8))
        ACT_BEFORE = {T_Z: 0, T_PATT: 36, T_GLU: 36, T_PSSM: 44, T_WOUT: 44, T_XK: 52, T_XQ: 68, T_XO: 76, T_FF: 76}
        DVE_BEFORE = {T_Z: 0, T_PATT: 0, T_GLU: 8, T_PSSM: 8, T_WOUT: 16, T_XK: 16, T_XQ: 16, T_XO: 16, T_FF: 24}
        N_SQ = 8

        block = ctx.enter_context(nc.Block())

        @block.sync
        def _(sp):
            def load_w(t, s, src):
                if not isinstance(t, int) or t >= 2:
                    sp.wait_ge(wl_done, t - 1)
                sp.dma_start(wraw[s][:], src).then_inc(w_loaded[s], 16)

            for i, (t0, n) in enumerate(tok):
                src = a["x_prompt"][0, t0:t0 + n, :] if i < 4 else a["x_sample"][0]
                sp.dma_start(xin[0:n, i, :], src).then_inc(x_loaded[i], 16)
                if i < 4:
                    sp.dma_start(vecs[8 * i + 32:8 * i + 40, :],
                                 a[VEC_ROWS[4 + i]][0].rearrange("(k c) -> k c", c=P)).then_inc(vecs_loaded, 16)
            for t in range(2):
                load_w(t, t, w_of["w_in"][:, :, t * P:(t + 1) * P])
            for i, name in enumerate(("ssm_a_re", "ssm_a_im", None, "state_ssm_re", "state_ssm_im")):
                if name:
                    src = a[name][0] if len(a[name].shape) == 3 else a[name][0, 0]
                    sp.dma_start(st5[:, i, :], src.rearrange("(r g) p -> r (g p)", g=2)).then_inc(st5_loaded, 16)
            sp.dma_start(dz[0:PAIRS, 31, 0:2], a["ssm_log_dt"][0].rearrange("(r g) -> r g", g=2)).then_inc(st5_loaded, 16)
            for c, name in enumerate(("ssm_c_re", "ssm_c_im")):
                sp.dma_start(craw[:, c], a[name][0].rearrange("g k p -> (g k) p").rearrange("(t r) p -> r t p", r=P)) \
                  .then_inc(c_loaded, 16)
            sp.dma_start(braw[:, 0], a["ssm_b_re"][0].rearrange("(r g) p k -> r (g p) k", g=2)).then_inc(b_loaded, 16)
            sp.dma_start(braw[:, 1], a["ssm_b_im"][0].rearrange("(r g) p k -> r (g p) k", g=2)).then_inc(b_loaded, 16)
            for t in range(2, 10):
                load_w(t, t % 2, w_of["w_in"][:, :, t * P:(t + 1) * P])
            for n, win in enumerate(("k", "v")):
                sp.dma_start(a[f"win_{win}_sample"][0, 0, 0:64].rearrange("w h d -> w (h d)"),
                             a[f"cache_win_{win}"][0, 0, 64:128].rearrange("w h d -> w (h d)")).then_inc(stored, 16)
            sp.wait_ge(xt_cp, 10)
            sp.dma_start(x_copy, x[:].rearrange("p k c -> p (k c)")).then_inc(x_spilled, 16)
            with sp.Fori(5, 18) as i:
                for j in range(2):
                    load_w(2 * i + j, j, w_of["w_in"][:, :, ds(256 * i + j * P, P)])
            for t0, name in ((T_PATT, "p_att"), (T_GLU, "w_glu"), (T_PSSM, "p_ssm"), (T_WOUT, "w_out"), (T_XK, "w_xk"),
                             (T_XV, "w_xv"), (T_XQ, "w_xq"), (T_XO, "w_xo")):
                for j in range(8):
                    load_w(t0 + j, j % 2, w_of[name][:, :, j * P:(j + 1) * P])
                    if t0 == T_PATT and j >= 3:
                        load_gate = j - 3
                        if load_gate == 0:
                            for s in range(2):
                                sp.wait_ge(gate_stored[s], 16 * 8)
                            sp.wait_ge(att_done, 9)
                            sp.wait_ge(y_ps, 8)
                            sp.dma_start(x[:].rearrange("p k c -> p (k c)"), x_copy).then_inc(x_back, 16)
                        if load_gate >= 2:
                            sp.wait_ge(gsig_ready, load_gate - 1)
                        sp.dma_start(gate[:, load_gate % 2], gates[8 + load_gate]).then_inc(gate_loaded[load_gate % 2], 16)
                    if t0 == T_GLU and j < 7:
                        n = 5 + j
                        sp.wait_ge(gsig_ready, n - 1)
                        sp.dma_start(gate[:, n % 2], gates[8 + n if n < 8 else n - 8]).then_inc(gate_loaded[n % 2], 16)
                    if (t0 == T_PSSM and j >= 6) or (t0 == T_WOUT and j < 2):
                        n = (6 + j if t0 == T_PSSM else 14 + j)
                        sp.wait_ge(gsig_ready, n - 1)
                        sp.dma_start(gate[:, n % 2], gates[n - 8]).then_inc(gate_loaded[n % 2], 16)
                    if t0 == T_WOUT and j in (3, 6):
                        i = j // 3 - 1
                        if i == 0:
                            sp.wait_ge(evac_dve, 16)
                        else:
                            sp.wait_ge(memr_used, 1)
                        sp.dma_start(memr[:], a["mem_prompt"][0, i * P:(i + 1) * P, :]).then_inc(mem_loaded[i], 16)
                    if t0 == T_XK and j == 4:
                        sp.wait_ge(gemm_done, T_XK)
                        sp.dma_start(smk[:], a["cache_mem_k"][0, 0].rearrange("(m p) h d -> p m (h d)", p=P)).then_inc(smk_loaded, 16)
                        sp.dma_start(smv[:], a["cache_mem_v"][0, 0].rearrange("(m p) h d -> p m (h d)", p=P)).then_inc(smv_loaded, 16)
            with sp.Fori(0, QUARTERS) as q:
                for j in range(8):
                    load_w(T_FF + 16 * q + j, j % 2, w_of["w_ff1"][:, :, ds(1024 * q + j * P, P)])
                for j in range(8):
                    load_w(T_FF + 8 + 16 * q + j, j % 2, w_ff2[:, ds(8 * q, 8), j * P:(j + 1) * P])
            for h in range(2):
                sp.wait_ge(yt_cp, 4 * (h + 1))
                c = slice(512 * h, 512 * (h + 1))
                sp.dma_start(a["y_prompt"][0].rearrange("(t p) c -> p t c", p=P)[:, :, c], yst[:, 0:4, c]).then_inc(stored, 16)
                sp.dma_start(a["y_sample"][0][:, c], yst[0:TS, 4, c]).then_inc(stored, 16)
            sp.wait_ge(stored, 16 * 6)
            sp.wait_ge(state_stored, 16 * 8)
            sp.wait_ge(mem_stored, 16 * 2)

        @block.gpsimd
        def _(pool):
            seq = Chain(pool, pool_seq)
            g = nc.gpsimd
            g.iota(cidi[:, 0:NBP], pattern=[[1, NBP]], base=0, channel_multiplier=0)
            seq(g.iota(cidi[:, NBP:NB], pattern=[[1, NB - NBP]], base=0, channel_multiplier=0))
            seq(g.tensor_copy(cidx[:], cidi[:]))
            seq(g.tensor_scalar(cmask[:], cidx[:], 1.0, 0.0, ALU.min, ALU.add))
            seq(g.memset(ident[:], 0.0))
            g.affine_select(out=ident[:], in_=ident[:], compare_op=ALU.not_equal, fill=1.0, base=0,
                            pattern=[[-1, P]], channel_multiplier=1).then_inc(const_ready, 1)
            g.memset(xm[:], 0.0)
            g.memset(zm[0][:], 0.0)
            g.memset(toep[0][:], 0.0)
            seq(g.memset(fin[:], 0.0))

            def bk(ap, shape):
                return ap.unsqueeze(len(ap.shape)).broadcast_to(shape)

            def phase_args(m):
                sh = [P, PB, NB]
                th = bk(thl[:, 0, ds(PB * m, PB)], sh)
                tl = bk(thl[:, 1, ds(PB * m, PB)], sh)
                ci = cidx[:].unsqueeze(1).broadcast_to(sh)
                e0 = earg[:, 0].rearrange("p (j c) -> p j c", j=PB)
                e1 = earg[:, 1].rearrange("p (j c) -> p j c", j=PB)
                seq(g.tensor_tensor(e0, ci, th, ALU.mult))
                seq(g.tensor_scalar(e1, e0, MAGIC, 1.0, ALU.add, ALU.mult))
                seq(g.tensor_scalar(e1, e1, -MAGIC, 1.0, ALU.add, ALU.mult))
                seq(g.tensor_tensor(e0, e0, e1, ALU.subtract))
                seq(g.tensor_tensor(e1, ci, tl, ALU.mult))
                g.tensor_tensor(e0, e0, e1, ALU.add).then_inc(earg_ready, 1)

            def in_table(m):
                pool.wait_ge(tab_ps, m)
                sh = [P, PB, SB, 16]
                for c, (f0, f1, op) in enumerate(((0, 1, ALU.subtract), (1, 0, ALU.add))):
                    for i, (f, b) in enumerate(((f0, 0), (f1, 1))):
                        fa = fb[:, f, :, ds(PB * m, PB)].rearrange("p s j -> p j s").unsqueeze(3).broadcast_to(sh)
                        ba = btab[:, b, :, ds(PB * m, PB)].rearrange("p k j -> p j k").unsqueeze(2).broadcast_to(sh)
                        last = g.tensor_tensor(prod[:, i, :, 0:SB, :], fa, ba, ALU.mult)
                    seq(last)
                    for h in range(2):
                        r = slice(64 * h, 64 * h + 64)
                        seq(g.tensor_tensor(xm[r, c, :, :, 16 * h:16 * h + 16], prod[r, 0, :, 0:SB, :],
                                            prod[r, 1, :, 0:SB, :], op))

            def out_table(m):
                if m >= 2:
                    pool.wait_ge(y_ps, m - 1)
                zb = zm[m % 2]
                sh = [P, PB, SB + 1, 16]
                sets = (((pw[:, 0], 0), (pw[:, 1], 1), ALU.subtract), ((npwi[:], 0), (pw[:, 0], 1), ALU.subtract))
                for c, (f0, f1, op) in enumerate(sets):
                    for i, (f, b) in enumerate((f0, f1)):
                        fa = f[:, :, ds(PB * m, PB)].rearrange("p s j -> p j s").unsqueeze(3).broadcast_to(sh)
                        ca = ctab[:, b, ds(PB * m, PB), :].unsqueeze(2).broadcast_to(sh)
                        last = g.tensor_tensor(prod[:, i], fa, ca, ALU.mult)
                    seq(last)
                    for h in range(2):
                        r = slice(64 * h, 64 * h + 64)
                        last = g.tensor_tensor(zb[r, c, :, :, 16 * h:16 * h + 16], prod[r, 0], prod[r, 1], op)
                        if (c, h) != (1, 1):
                            seq(last)
                last.then_inc(tab_ready, 1)
                pool.wait_ge(tab_ready, m + 1)

            def e_table(m):
                if m >= 2:
                    pool.wait_ge(h_ready, m - 1)
                eim, erm = ei[m % 2], er[m % 2]
                pool.wait_ge(trig_ready, m + 1)
                e0 = earg[:, 0].rearrange("p (j c) -> p j c", j=PB)
                e1 = earg[:, 1].rearrange("p (j c) -> p j c", j=PB)
                g.tensor_tensor(eim[:], e0, e1, ALU.mult)
                seq(g.tensor_tensor(erm[:], e0, e0, ALU.mult))
                g.tensor_scalar(eim[:], eim[:], 2.0, 0.0, ALU.mult, ALU.add)
                g.tensor_scalar(erm[:], erm[:], -2.0, 1.0, ALU.mult, ALU.add)
                g.tensor_tensor(rho[m % 2][:], bk(thl[:, 2, ds(PB * m, PB)], [P, PB, NB]),
                                cmask[:].unsqueeze(1).broadcast_to([P, PB, NB]), ALU.mult).then_inc(e_ready, 1)
                pool.wait_ge(e_ready, m + 1)

            pool.wait_ge(coef_ready, 1)
            pool.wait_ge(st_cp, 3)
            pool.wait_ge(in_h, KT)
            phase_args(0)
            for m in range(PAIRS // PB):
                in_table(m)
                if m == 1:
                    pool.wait_ge(x_spilled, 16)
                    g.memset(toep[1][:], 0.0)
                    seq(g.memset(zm[1][:], 0.0))
                out_table(m)
                e_table(m)
                if m < 7:
                    phase_args(m + 1)
            pool.wait_ge(gemm_done, T_PATT)
            for j in range(2):
                r = slice(64 * j, 64 * j + 64)
                seq(g.iota(disti[r, :], pattern=[[-1, 192]], base=2 * CH, channel_multiplier=1))
            g.tensor_copy(dist[:], disti[:]).then_inc(dist_ready, 1)
            g.memset(qc[0][:], 0.0)
            seq(g.memset(qc[1][:], 0.0))

            def queries(n, b):
                if not isinstance(n, int) or n >= 2:
                        pool.wait_ge(s_ps, n - 1)
                for half in range(2):
                    for par in range(2):
                        src = z[64 * par:64 * par + 64, 8:16, ds(CH * n, CH)] \
                            .rearrange("p (s h j) q -> p h s j q", s=2, j=2)[:, half]
                        dst = qc[b][64 * half:64 * half + 64].rearrange("p (s h a) j q -> p h a s j q", s=2, h=2)[:, half, par]
                        last = g.tensor_copy(dst, src)
                        if (half, par) != (1, 1):
                            seq(last)
                last.then_inc(qc_ready, 1)
                pool.wait_ge(qc_ready, n + 1)

            for n in range(9):
                queries(n, n % 2)

        @block.scalar
        def _(act):
            seq = Chain(act, act_seq)
            s_ = nc.scalar

            def split_h(t, j):
                w, s = j % 2, j % 4
                act.wait_ge(w_loaded[w], 8 * (t - w) + 16)
                if not isinstance(t, int) or t >= 4:
                    act.wait_ge(gemm_done, t - 3)
                s_.activation(wH[s][:], wraw[w][:], ACT.Copy).then_inc(wh_done, 1)

            def result(j):
                return gp[:, 2 * (j % 2):2 * (j % 2) + 2, 0:HT]

            def halves(ap):
                return ap.rearrange("p (h c) -> p h c", h=2)

            for i, name in enumerate(VEC_ROWS[0:4]):
                act.dma_start(vecs[8 * i:8 * i + 8, :], a[name][0].rearrange("(k c) -> k c", c=P)).then_inc(vecs_loaded, 16)

            act.wait_ge(ones_ready, 1)

            def row_root(i):
                n = tok[i][1]
                act.wait_ge(x_loaded[i], 16)
                seq(s_.activation(xsq[i][0:n, :], xin[0:n, i, :], ACT.Square, accum_out=xss[0:n, 0, i:i + 1]))
                s_.activation(xss[0:n, 1, i:i + 1], xss[0:n, 0, i:i + 1], ACT.Sqrt, bias=eps[0:n, 0:1], scale=1.0 / D) \
                  .then_inc(xr_ready, 1)

            def row_h(i):
                t0, n = tok[i]
                act.wait_ge(xnt_ps, i + 1)
                for k in range(KT):
                    last = s_.activation(aH[:, k, t0:t0 + n], sp_[:, (2 * i + k // 4) % 4, (k % 4) * P:(k % 4) * P + n],
                                         ACT.Copy, scale=gains[:, 8 * G_MIX_PRE + k:8 * G_MIX_PRE + k + 1])
                last.then_inc(xh_done, 1) if i < 4 else last.then_inc(in_h, KT)

            row_root(0)
            row_root(1)
            act.wait_ge(g_ps, 1)
            s_.activation(gains[:], sp_[:, 3, 0:64], ACT.Copy).then_inc(g_cp, 1)
            act.wait_ge(g_cp, 1)
            for i in range(5):
                row_h(i)
                if i < 3:
                    row_root(i + 2)
                if i in (1, 2):
                    split_h(i - 1, i - 1)
            split_h(2, 2)

            n_sq = [0]

            def square(src, k):
                if n_sq[0] >= 2:
                    act.wait_ge(sq_used, n_sq[0] - 1)
                s_.activation(sq[:, k % 2], src, ACT.Square).then_inc(sq_ready, 1)
                n_sq[0] += 1

            def root(n):
                act.wait_ge(sq_used, 8 * n)
                s_.activation(halves(rstd[:]), sp_[:, 0:2, 0:HT], ACT.Sqrt, bias=eps[:, 0:1], scale=1.0 / D) \
                  .then_inc(root_ready, 1)

            n_raw = [0]

            def cut_h(dst, src):
                n_raw[0] += 1
                act.wait_ge(raw_ready, n_raw[0])
                s_.activation(dst, src, ACT.Copy).then_inc(in_h, 1)

            def evac_z(t, j):
                act.wait_ge(gemm_done, t + 1)
                dst = halves(z[:, t, :]) if isinstance(t, int) else halves(z[:, ds(t, 1), :].rearrange("p o c -> p (o c)"))
                s_.activation(dst, result(j), ACT.Copy).then_inc(evac_act, 1)

            for t in range(8):
                split_h(t + AHEAD, t + AHEAD)
                if t == 0:
                    act.wait_ge(st_ps, 1)
                    s_.activation(dz[:, 0:5, :], sp_[:, 3, 0:160].rearrange("p (i r) -> p i r", i=5), ACT.Copy).then_inc(st_cp, 1)
                if t == 1:
                    act.wait_ge(st_ps, 2)
                    for c in range(2):
                        for q in range(2):
                            src = sp_[0:64, 2 * c + q, :].rearrange("p (r g k) -> p g r k", g=2, k=16)
                            for h in range(2):
                                last = s_.activation(ctab[64 * h:64 * h + 64, c, 16 * q:16 * q + 16, :], src[:, h], ACT.Copy)
                    last.then_inc(st_cp, 1)
                    act.wait_ge(st_cp, 2)
                    s_.activation(dz[:, 5], dz[:, 2], ACT.Exp).then_inc(disc_a, 1)
                if t == 2:
                    act.wait_ge(st_ps, 3)
                    s_.activation(btab[:].rearrange("p c k r -> p c (k r)"), sp_[:, 0:2, :], ACT.Copy).then_inc(st_cp, 1)
                    act.wait_ge(disc_v, 1)
                    s_.activation(dz[:, 10], dz[:, 6], ACT.Exp)
                    s_.activation(thl[:, 2], dz[:, 6], ACT.Exp, scale=4.0)
                    s_.activation(dz[:, 11], dz[:, 8], ACT.Sin, scale=0.5)
                    s_.activation(dz[:, 12], dz[:, 9], ACT.Sin, scale=-0.5, bias=halfpi[:, 0:1]).then_inc(disc_a, 1)
                evac_z(t, t)
                for i in {3: (0, 1), 4: (2, 3), 5: (4,)}.get(t, ()):
                    t0, n = tok[i]
                    for kh in range(2):
                        act.wait_ge(xt_ps, 2 * i + kh + 1)
                        src = sp_[:, (2 * i + kh) % 4, :].rearrange("p (k c) -> p k c", k=4)[:, :, 0:n]
                        s_.activation(x[:, 4 * kh:4 * kh + 4, t0:t0 + n], src, ACT.Copy).then_inc(xt_cp, 1)

            def trig(m):
                act.wait_ge(earg_ready, m + 1)
                seq(s_.activation(earg[:, 1], earg[:, 0], ACT.Abs))
                s_.activation(earg[:, 1], earg[:, 1], ACT.Sin, scale=-math.pi, bias=halfpi[:, 0:1])
                s_.activation(earg[:, 0], earg[:, 0], ACT.Sin, scale=math.pi).then_inc(trig_ready, 1)

            trig(0)

            def u_build(m, b):
                if not isinstance(m, int) or m >= 1:
                    act.wait_ge(v_ps, m)
                act.wait_ge(evac_act, 8)
                for j in range(PB):
                    src = z[32 * j:32 * j + 32, ds(m, 1), :].rearrange("p o (c s) -> p (o s) c", s=SB)
                    for s in range(SB):
                        last = s_.activation(ub[b][32 * s:32 * s + 32, j, :], src[:, s], ACT.Copy)
                last.then_inc(u_built, 1)

            def xt_copy(m):
                act.wait_ge(tab_ps, m + 1)
                s_.activation(xt[:].rearrange("p c j q -> p c (j q)"), sp_[:, 0:2, :], ACT.Copy).then_inc(xtab_cp, 1)

            def evac_gate(t, j, n):
                act.wait_ge(gemm_done, t + 1)
                if not isinstance(n, int) or n >= 2:
                    act.wait_ge(gate_stored[j % 2], 8 * (n - j % 2))
                s_.activation(halves(sq[:, j % 2]), result(j), ACT.Copy).then_inc(evac_act, 1)
                act.wait_ge(evac_act, t + 1)
                act.dma_start(gates[ds(n, 1)].rearrange("o p c -> p (o c)"), sq[:, j % 2]).then_inc(gate_stored[j % 2], 16)

            def ssm_step(m, slabs, spill):
                for i, t in enumerate(slabs):
                    split_h(t + AHEAD, t + AHEAD)
                    if i == 0:
                        u_build(m + 1, (m + 1) % 2)
                    if i == len(slabs) - 1 and m < 6:
                        trig(m + 2)
                    if spill:
                        evac_gate(t, t, t - 20)
                    else:
                        evac_z(t, t)
                    if i == len(slabs) // 2 - 1:
                        xt_copy(m + 1)

            for m in range(-1, 7):
                ssm_step(m, SSM_SLABS[m], m >= 2)

            act.wait_ge(tab_ps, 8)
            act.dma_start(cv[:], a["cache_win_v"][0, 0].rearrange("w h d -> w (h d)")).then_inc(cache_loaded, 16)
            act.dma_start(ck[:], a["cache_win_k"][0, 0].rearrange("w h d -> w (h d)")).then_inc(cache_loaded, 16)
            with nc.allow_non_contiguous_dma(reason="16 sinks, once"):
                for j in range(2):
                    src = a["attn_sinks"][0].rearrange("(r j p) -> j r p", j=2, p=2)[j]
                    act.dma_start(sink[64 * j:64 * j + 64, :].rearrange("q (r p) -> q r p", p=2),
                                  src.partition_broadcast(64)).then_inc(sink_loaded, 16)
            for i in range(5):
                act.wait_ge(va_ps, i + 1)
                n = 2 if i < 4 else 1
                rows_ = P if i < 4 else TS
                s_.activation(vp[0:rows_, 2 * i:2 * i + n, :],
                              gp[0:rows_, i % 4, 0:n * KV].rearrange("p (i c) -> p i c", i=n), ACT.Copy).then_inc(va_cp, 1)
            act.wait_ge(va_ps, 6)
            s_.activation(kout[:, 0, :], gp[:, 1, 0:KV], ACT.Copy)
            s_.activation(kout[0:TS, 1, :], gp[0:TS, 1, KV:2 * KV], ACT.Copy)
            s_.activation(ks[:, :, 0:128], gp[:, 2, 0:256].rearrange("p (h c) -> p h c", h=2), ACT.Copy)
            s_.activation(ks[:, :, 128:192], z[:, 16:18, TP:TT], ACT.Copy).then_inc(va_cp, 1)
            act.wait_ge(va_ps, 7)
            s_.activation(fout[:], sp_[0:PAIRS, 3, :].rearrange("p (i c) -> p i c", i=4), ACT.Copy).then_inc(va_cp, 1)
            act.wait_ge(va_cp, 7)
            flat = "w h d -> w (h d)"
            act.dma_start(a["win_k_prompt"][0, 0].rearrange(flat), kout[:, 0, :]).then_inc(state_stored, 16)
            act.dma_start(a["win_k_sample"][0, 0, 64:128].rearrange(flat), kout[0:TS, 1, :]).then_inc(state_stored, 16)
            act.dma_start(a["win_v_prompt"][0, 0].rearrange(flat), vp[:, 6, :]).then_inc(state_stored, 16)
            act.dma_start(a["win_v_sample"][0, 0, 64:128].rearrange(flat), vp[0:TS, 8, :]).then_inc(state_stored, 16)
            for i, name in enumerate(("ssm_re_prompt", "ssm_im_prompt", "ssm_re_sample", "ssm_im_sample")):
                act.dma_start(a[name][0, 0].rearrange("(r g) p -> r (g p)", g=2), fout[:, i, :]).then_inc(state_stored, 16)

            def soften(n, b, c0):
                act.wait_ge(m_ready, n + 1)
                for i in range(8):
                    last = s_.activation(sc[b][:, i, c0:192], sc[b][:, i, c0:192], ACT.Exp, bias=negm[:, b, i:i + 1],
                                         accum_out=den[:, b, i:i + 1])
                last.then_inc(p_ready, 1)
                s_.activation(esink[:, b, :], esink[:, b, :], ACT.Exp).then_inc(es_ready, 1)

            def turned(n):
                act.wait_ge(ot_ps, n + 1)
                s_.activation(z[:, 8:16, ds(CH * n, CH)], sp_[:, 3, :].rearrange("p (i c) -> p i c", i=8), ACT.Copy) \
                  .then_inc(att_done, 1)

            def band_step(n, b, wide=True, before=True, c0=0):
                for h in range(2):
                    if wide:
                        act.wait_ge(pt_ps, 2 * n + h + 1)
                        s_.activation(pta[b][:, 4 * h:4 * h + 4, :],
                                      sp_[:, 0, :].rearrange("p (i c) -> p i c", i=4), ACT.Copy).then_inc(pta_cp, 1)
                    if h == 0 and before:
                        turned(n - 1)
                if c0 is not None:
                    soften(n + 1, 1 - b, c0)

            soften(0, 0, 128)
            band_step(0, 0, wide=False, before=False, c0=64)
            band_step(1, 1)
            with act.Fori(1, 3) as i:
                for b in range(2):
                    band_step(2 * i + b, b)
            band_step(6, 0)
            band_step(7, 1)
            band_step(8, 0, c0=None)
            turned(8)

            act.wait_ge(att_done, 9)
            act.wait_ge(state_stored, 16 * 8)
            for k in range(KT):
                s_.activation(aH[:, k, :], z[:, 8 + k, :], ACT.Copy).then_inc(in_h, 1)

            def gate_sig(n):
                act.wait_ge(gate_loaded[n % 2], 16 * (n // 2 + 1))
                if n >= 2:
                    act.wait_ge(evac_dve, n - 1)
                s_.activation(gsig[:, n % 2], gate[:, n % 2], ACT.Sigmoid).then_inc(gsig_ready, 1)

            for j in range(8):
                split_h(T_PATT + j + AHEAD, j + AHEAD)
                if j == 0:
                    gate_sig(0)
                    act.wait_ge(y_evac, 9)
                    for k in range(KT):
                        s_.activation(z[:, k, :], z[:, k, :], ACT.Gelu_apprx_tanh).then_inc(gelu_done, 1)
                    act.wait_ge(gelu_done, 8)
                s_.activation(bH[:, j, :], z[:, j, :], ACT.Copy).then_inc(in_h, 1)
                if j:
                    gate_sig(j)
            for j in range(8):
                split_h(T_GLU + j + AHEAD, j + AHEAD)
                act.wait_ge(gemm_done, T_GLU + j + 1)
                s_.activation(halves(raw[:, j % 2]), result(j), ACT.Sigmoid).then_inc(evac_act, 1)
                cut_h(aH[:, j, :], sq[:, j % 2])
                if j in (1, 2):
                    gate_sig(7 + j)
            for j in range(8):
                split_h(T_PSSM + j + AHEAD, j + AHEAD)
                if 1 <= j < 7:
                    gate_sig(9 + j)
                cut_h(bH[:, j, :], raw[:, j % 2])

            def mem_norm(i):
                act.wait_ge(mem_loaded[i], 16)
                if i == 1:
                    act.wait_ge(mm_ps, 1)
                seq(s_.activation(memn[:], memr[:], ACT.Square, accum_out=memss[:, i:i + 1]))
                s_.activation(memss[:, 2 + i:3 + i], memss[:, i:i + 1], ACT.Sqrt, bias=eps[:, 0:1], scale=1.0 / D) \
                  .then_inc(mn_ready, 1)

            def mem_cut(i):
                act.wait_ge(mm_ps, i + 1)
                for k in range(KT):
                    last = s_.activation(mmH[:, k, i * P:(i + 1) * P], sp_[:, 2 + k // 4, (k % 4) * P:(k % 4 + 1) * P],
                                         ACT.Copy, scale=gains[:, 8 * G_MEM + k:8 * G_MEM + k + 1])
                last.then_inc(mmh_done, 1)

            for j in range(8):
                t = T_WOUT + j
                split_h(t + AHEAD, j + AHEAD)
                act.wait_ge(gemm_done, t + 1)
                s_.activation(halves(o[:, j, :]), result(j), ACT.Copy).then_inc(evac_act, 1)
                act.wait_ge(evac_act, ACT_BEFORE[T_WOUT] + j + 1)
                square(o[:, j, :], j)
                if j in (2, 5):
                    mem_norm(j // 3)
                if j in (4, 7):
                    mem_cut((j - 4) // 3)
            root(1)

            def evac_mem(t, j):
                act.wait_ge(gemm_done, t + 1)
                if t >= T_XV + 2:
                    act.wait_ge(kvt_ps, t - T_XK - 1)
                dst = mkT[:, j, :] if t < T_XV else mvT[:, j % 2, :]
                s_.activation(dst, gp[:, 2 * (j % 2), 0:NMEM], ACT.Copy).then_inc(evac_act, 1)

            for j in range(16):
                t = T_XK + j
                split_h(t + AHEAD, j + AHEAD)
                if 1 <= j <= KT:
                    act.wait_ge(x_done, j)
                    square(x[:, j - 1, :], j - 1)
                evac_mem(t, j % 8)
                if j == KT:
                    root(2)
                if j > KT:
                    cut_h(aH[:, j - KT - 1, :], raw[:, (j - KT - 1) % 2, :])
            cut_h(aH[:, KT - 1, :], raw[:, (KT - 1) % 2, :])

            for i in range(4):
                act.wait_ge(smk_ps, i + 1)
                s_.activation(smkT[:, 2 * i:2 * i + 2, :],
                              sp_[:, 2 + i % 2, :].rearrange("p (k c) -> p k c", k=2), ACT.Copy).then_inc(smk_cp, 1)
            act.wait_ge(kvt_cp, 16)
            act.dma_start(a["mem_k_prompt"][0, 0].rearrange("(m p) h d -> p m (h d)", p=P), mk[:]).then_inc(mem_stored, 16)
            act.dma_start(a["mem_v_prompt"][0, 0].rearrange("(m p) h d -> p m (h d)", p=P), mv[:]).then_inc(mem_stored, 16)

            for j in range(8):
                t = T_XQ + j
                split_h(t + AHEAD, j + AHEAD)
                act.wait_ge(gemm_done, t + 1)
                s_.activation(halves(xq[:, j, :]), result(j), ACT.Copy).then_inc(evac_act, 1)

            def cross_soft(i):
                n = tok[i][1]
                act.wait_ge(xm_ready, i + 1)
                if i >= 2:
                    act.wait_ge(xpt_ps, 2 * i - 2)
                for h in range(4):
                    last = s_.activation(pc[i % 2][0:n, h, :], gp[0:n, 2 * (i % 2) + h // 2, (h % 2) * NMEM:(h % 2 + 1) * NMEM],
                                         ACT.Exp, bias=negm[0:n, i % 2, h:h + 1], scale=1.0 / 16,
                                         accum_out=den[0:n, i % 2, h:h + 1])
                last.then_inc(xp_ready, 1)

            def cross_out(i):
                t0, n = tok[i]
                act.wait_ge(xpt_ps, 2 * i + 1)
                if i >= 1:
                    act.wait_ge(xo_ps, i)
                s_.activation(ptc[:, 0:2, :, 0:n].rearrange("p h m q -> p (h m) q"),
                              sp_[:, 0, :].rearrange("p (i q) -> p i q", i=4)[:, :, 0:n], ACT.Copy).then_inc(xpt_cp, 1)
                act.wait_ge(xpt_ps, 2 * i + 2)
                s_.activation(ptc[:, 2:4, :, 0:n].rearrange("p h m q -> p (h m) q"),
                              sp_[:, 1, :].rearrange("p (i q) -> p i q", i=4)[:, :, 0:n], ACT.Copy).then_inc(xpt_cp, 1)
                if i < 3:
                    cross_soft(i + 2)
                act.wait_ge(xo_ps, i + 1)
                s_.activation(aH[:, :, t0:t0 + n].rearrange("p (b k) q -> p b k q", b=2),
                              sp_[:, 2:4, :].rearrange("p b (k q) -> p b k q", k=4)[:, :, :, 0:n], ACT.Copy).then_inc(ca_h, 1)

            cross_soft(0)
            cross_soft(1)
            for i in range(5):
                cross_out(i)

            for j in range(8):
                split_h(T_XO + j + AHEAD, j + AHEAD)
                act.wait_ge(evac_dve, DVE_BEFORE[T_XO] + j + 1)
                square(o[:, j, :], j)
            root(3)
            for k in range(KT):
                act.wait_ge(x_done, 8 + k + 1)
                square(x[:, k, :], k)
            root(4)
            for k in range(KT):
                cut_h(aH[:, k, :], raw[:, k % 2, :])

            def ff(q, last_one):
                for j in range(8):
                    t = T_FF + 16 * q + j
                    split_h(t + AHEAD, j + AHEAD)
                    act.wait_ge(gemm_done, t + 1)
                    s_.activation(halves(raw[:, j % 2]), result(j), ACT.Relu).then_inc(evac_act, 1)
                    act.wait_ge(raw_ready, n_raw[0] + 8 * q + j + 1)
                    s_.activation(bH[:, j, :], sq[:, j % 2], ACT.Copy).then_inc(in_h, 1)
                for j in range(8):
                    t = T_FF + 8 + 16 * q + j
                    if not last_one or j + AHEAD < 8:
                        split_h(t + AHEAD, j + AHEAD)
                    if last_one:
                        act.wait_ge(evac_dve, DVE_BEFORE[T_FF] + 8 * q + j + 1)
                        square(o[:, j, :], j)

            act.wait_ge(mem_stored, 16 * 2)
            with act.Fori(0, QUARTERS - 1) as q:
                ff(q, False)
            ff(QUARTERS - 1, True)
            root(5)
            for k in range(KT):
                act.wait_ge(yt_ps, k + 1)
                s_.activation(yst[:, 0:4, k * P:(k + 1) * P],
                              sp_[:, 2 * (k % 2), :].rearrange("p (t c) -> p t c", t=4), ACT.Copy)
                s_.activation(yst[0:TS, 4, k * P:(k + 1) * P], sp_[0:TS, 2 * (k % 2) + 1, 0:P], ACT.Copy).then_inc(yt_cp, 1)

        @block.vector
        def _(dve):
            seq = Chain(dve, dve_seq)
            v = nc.vector

            def split_l(t, j):
                w, s = j % 2, j % 4
                dve.wait_ge(wh_done, t + 1)
                v.tensor_tensor(wL[s][:], wraw[w][:], wH[s][:], ALU.subtract).then_inc(wl_done, 1)

            def result(j):
                return gp[:, 2 * (j % 2):2 * (j % 2) + 2, 0:HT]

            def halves(ap):
                return ap.rearrange("p (h c) -> p h c", h=2)

            n_in = [0]

            def cut_l(dst, src, h):
                n_in[0] += 1
                dve.wait_ge(in_h, n_in[0])
                v.tensor_tensor(dst, src, h, ALU.subtract).then_inc(in_l, 1)

            v.memset(eps[:], EPS)
            v.memset(halfpi[:], math.pi / 2)
            v.memset(ones[:], 1.0).then_inc(ones_ready, 1)

            def row_scale(i):
                n = tok[i][1]
                dve.wait_ge(xr_ready, i + 1)
                seq(v.reciprocal(xss[0:n, 2, i:i + 1], xss[0:n, 1, i:i + 1]))
                if i >= 2:
                    dve.wait_ge(xnt_ps, i - 1)
                v.tensor_scalar(xn[0:n, i % 2], xin[0:n, i], xss[0:n, 2, i:i + 1], None, ALU.mult).then_inc(xnt_ready, 1)

            def row_l(i):
                t0, n = tok[i]
                if i == 0:
                    dve.wait_ge(g_cp, 1)
                dve.wait_ge(xh_done, i + 1) if i < 4 else dve.wait_ge(in_h, KT)
                for k in range(KT):
                    last = v.scalar_tensor_tensor(aL[:, k, t0:t0 + n], sp_[:, (2 * i + k // 4) % 4, (k % 4) * P:(k % 4) * P + n],
                                                  gains[:, 8 * G_MIX_PRE + k:8 * G_MIX_PRE + k + 1], aH[:, k, t0:t0 + n],
                                                  ALU.mult, ALU.subtract)
                last.then_inc(xl_done, 1) if i < 4 else last.then_inc(in_l, KT)

            row_scale(0)
            for i in range(5):
                if i < 4:
                    row_scale(i + 1)
                if i in (2, 3):
                    split_l(i - 2, i - 2)
                row_l(i)
            n_in[0] = KT
            split_l(2, 2)
            dve.wait_ge(st5_loaded, 80)
            v.tensor_copy(st5[:, 2, :].rearrange("r (g p) -> r g p", g=2),
                          dz[0:PAIRS, 31, 0:2].unsqueeze(2).broadcast_to([PAIRS, 2, 64])).then_inc(dt_ready, 1)

            def inverse(n):
                dve.wait_ge(root_ready, n)
                seq(v.reciprocal(rstd[:], rstd[:]))

            def apply(gain, k):
                v.scalar_tensor_tensor(raw[:, k % 2, :], x[:, k, :], gains[:, 8 * gain + k:8 * gain + k + 1], rstd[:],
                                       ALU.mult, ALU.mult).then_inc(raw_ready, 1)

            def pre_norm(n, gain, between=None):
                inverse(n)
                for k in range(KT + 1):
                    if k < KT:
                        if k >= 2:
                            dve.wait_ge(in_l, n_in[0])
                        apply(gain, k)
                    if k:
                        cut_l(aL[:, k - 1, :], raw[:, (k - 1) % 2, :], aH[:, k - 1, :])
                    if between:
                        between(k)

            def post_norm(n, gain, between=None):
                inverse(n)
                for k in range(KT):
                    if k >= 2:
                        dve.wait_ge(x_done, 8 * (n // 2) + k - 1)
                    seq(v.scalar_tensor_tensor(raw[:, k % 2, :], o[:, k, :], gains[:, 8 * gain + k:8 * gain + k + 1],
                                               rstd[:], ALU.mult, ALU.mult))
                    if n == 1 and k == 0:
                        dve.wait_ge(x_back, 16)
                    v.tensor_tensor(x[:, k, :], x[:, k, :], raw[:, k % 2, :], ALU.add).then_inc(x_done, 1)
                    if between:
                        between(k)

            def d(i):
                return dz[:, i]

            def tt(out, x0, x1, op):
                seq(v.tensor_tensor(out, x0, x1, op))

            for t in range(8):
                split_l(t + AHEAD, t + AHEAD)
                if t == 1:
                    dve.wait_ge(disc_a, 1)
                    tt(d(6), d(5), d(0), ALU.mult)
                    tt(d(7), d(5), d(1), ALU.mult)
                    seq(v.tensor_scalar(d(13), d(7), 1.0 / TWO_PI, MAGIC, ALU.mult, ALU.add))
                    seq(v.tensor_scalar(d(13), d(13), MAGIC, None, ALU.subtract))
                    seq(v.scalar_tensor_tensor(d(8), d(13), -C1, d(7), ALU.mult, ALU.add))
                    seq(v.scalar_tensor_tensor(d(8), d(13), -C2, d(8), ALU.mult, ALU.add))
                    seq(v.scalar_tensor_tensor(d(8), d(13), -C3, d(8), ALU.mult, ALU.add))
                    seq(v.tensor_scalar(d(14), d(8), math.pi, -math.pi, ALU.min, ALU.max))
                    seq(v.tensor_copy(d(8), d(14)))
                    v.scalar_tensor_tensor(d(9), d(8), -1.0, d(8), ALU.mult, ALU.max).then_inc(disc_v, 1)
                    tt(d(14), d(0), d(0), ALU.mult)
                    tt(d(15), d(1), d(1), ALU.mult)
                    tt(d(14), d(14), d(15), ALU.add)
                    seq(v.reciprocal(d(16), d(14)))
                if t == 2:
                    tt_ = v.tensor_scalar(d(17), d(8), 4.0 / TWO_PI, None, ALU.mult)
                    seq(tt_)
                    seq(v.tensor_scalar(d(18), d(17), MAGIC, MAGIC, ALU.add, ALU.subtract))
                    tt(d(17), d(17), d(18), ALU.subtract)
                    seq(v.tensor_scalar(d(18), d(17), 2.0 ** 15, MAGIC, ALU.mult, ALU.add))
                    seq(v.tensor_scalar(thl[:, 0], d(18), MAGIC, 2.0 ** -15, ALU.subtract, ALU.mult))
                    tt(thl[:, 1], d(17), thl[:, 0], ALU.subtract)
                if t == 3:
                    dve.wait_ge(disc_a, 2)
                    tt(d(19), d(11), d(11), ALU.mult)
                    seq(v.tensor_scalar(d(19), d(19), -2.0, 1.0, ALU.mult, ALU.add))
                    tt(d(20), d(11), d(12), ALU.mult)
                    v.memset(pw[:, 0, 0, :], 1.0)
                    v.memset(pw[:, 1, 0, :], 0.0)
                    tt(pw[:, 0, 1, :], d(10), d(19), ALU.mult)
                    seq(v.scalar_tensor_tensor(pw[:, 1, 1, :], d(20), 2.0, d(10), ALU.mult, ALU.mult))
                    for n in range(2, 5):
                        tt(d(21), pw[:, 0, 1, :], pw[:, 0, n - 1, :], ALU.mult)
                        tt(d(22), pw[:, 1, 1, :], pw[:, 1, n - 1, :], ALU.mult)
                        tt(pw[:, 0, n, :], d(21), d(22), ALU.subtract)
                        tt(d(21), pw[:, 0, 1, :], pw[:, 1, n - 1, :], ALU.mult)
                        tt(d(22), pw[:, 1, 1, :], pw[:, 0, n - 1, :], ALU.mult)
                        tt(pw[:, 1, n, :], d(21), d(22), ALU.add)
                    seq(v.tensor_scalar(npwi[:], pw[:, 1], -1.0, None, ALU.mult))
                if t == 4:
                    seq(v.tensor_scalar(d(23), pw[:, 0, 1, :], 1.0, None, ALU.subtract))
                    tt(d(21), d(23), d(0), ALU.mult)
                    tt(d(22), pw[:, 1, 1, :], d(1), ALU.mult)
                    tt(d(24), d(21), d(22), ALU.add)
                    tt(d(24), d(24), d(16), ALU.mult)
                    tt(d(21), pw[:, 1, 1, :], d(0), ALU.mult)
                    tt(d(22), d(23), d(1), ALU.mult)
                    tt(d(25), d(21), d(22), ALU.subtract)
                    tt(d(25), d(25), d(16), ALU.mult)
                    for s in range(SB):
                        n = SB - 1 - s
                        tt(d(21), pw[:, 0, n, :], d(24), ALU.mult)
                        tt(d(22), pw[:, 1, n, :], d(25), ALU.mult)
                        tt(fb[:, 0, s, :], d(21), d(22), ALU.subtract)
                        tt(d(21), pw[:, 0, n, :], d(25), ALU.mult)
                        tt(d(22), pw[:, 1, n, :], d(24), ALU.mult)
                        tt(fb[:, 1, s, :], d(21), d(22), ALU.add)
                    seq(v.tensor_copy(init[:], dz[:, 3:5, :]))
                    tt(d(21), pw[:, 0, 4, :], init[:, 0], ALU.mult)
                    tt(d(22), pw[:, 1, 4, :], init[:, 1], ALU.mult)
                    tt(a4init[:, 0], d(21), d(22), ALU.subtract)
                    tt(d(21), pw[:, 0, 4, :], init[:, 1], ALU.mult)
                    tt(d(22), pw[:, 1, 4, :], init[:, 0], ALU.mult)
                    v.tensor_tensor(a4init[:, 1], d(21), d(22), ALU.add).then_inc(coef_ready, 1)
                    dve.wait_ge(st_ps, 3)
                    v.memset(hs[:, :, :, 0:1], 0.0).then_inc(y_evac, 1)

            def b4(ap, m):
                return ap[:, ds(PB * m, PB)].unsqueeze(2)

            def toep_out(m, b):
                dve.wait_ge(tab_ps, m + 1)
                ps = sp_[0:32, 2, :].rearrange("p (j c) -> p j c", j=PB)
                for s in range(SB):
                    last = v.tensor_copy(toep[b][32 * s:32 * s + 32, :, 32 * s:P], ps[:, :, 0:P - 32 * s])
                last.then_inc(toep_cp, 1)

            def turn_in(m, b):
                dve.wait_ge(v_ps, m + 1)
                dve.wait_ge(e_ready, m + 1)
                sh = "p j c -> p (j c)"
                vr = sp_[:, 0:2, 0:2 * NB]
                vi = sp_[:, 2:4, 0:2 * NB]
                e_r = er[b][:].rearrange(sh).rearrange("p (b c) -> p b c", b=2)
                e_i = ei[b][:].rearrange(sh).rearrange("p (b c) -> p b c", b=2)
                r = [rot[:, i].rearrange(sh).rearrange("p (b c) -> p b c", b=2) for i in range(4)]
                v.tensor_tensor(r[0], vr, e_r, ALU.mult)
                v.tensor_tensor(r[1], vi, e_i, ALU.mult)
                v.tensor_tensor(r[2], vi, e_r, ALU.mult)
                v.tensor_tensor(r[3], vr, e_i, ALU.mult).then_inc(v_read, 1)
                dve.wait_ge(v_read, m + 1)
                v.tensor_tensor(r[0], r[0], r[1], ALU.add)
                seq(v.tensor_tensor(r[2], r[2], r[3], ALU.subtract))
                for i, c in ((0, 0), (2, 1)):
                    w = rot[:, i, :, NBP:NBP + 1]
                    last = v.tensor_tensor(w, w, b4(a4init[:, c], m), ALU.add)
                seq(last)

            def scan_and_turn(m, b):
                sh = "p j c -> p (j c)"
                v.tensor_tensor_scan(rot[:, 1].rearrange(sh), rho[b][:].rearrange(sh), rot[:, 0].rearrange(sh), 0.0,
                                     ALU.mult, ALU.add)
                seq(v.tensor_tensor_scan(rot[:, 3].rearrange(sh), rho[b][:].rearrange(sh), rot[:, 2].rearrange(sh), 0.0,
                                         ALU.mult, ALU.add))
                v.tensor_tensor(rot[:, 0], rot[:, 1], er[b][:], ALU.mult)
                seq(v.tensor_tensor(rot[:, 2], rot[:, 3], ei[b][:], ALU.mult))
                v.tensor_tensor(hs[:, 0, :, 1:NB + 1], rot[:, 0], rot[:, 2], ALU.subtract)
                v.tensor_tensor(rot[:, 1], rot[:, 1], ei[b][:], ALU.mult)
                seq(v.tensor_tensor(rot[:, 3], rot[:, 3], er[b][:], ALU.mult))
                seq(v.tensor_tensor(hs[:, 1, :, 1:NB + 1], rot[:, 1], rot[:, 3], ALU.add))
                v.tensor_copy(fin[:, :, ds(PB * m, PB), 0:1], hs[:, :, :, NBP:NBP + 1])
                seq(v.tensor_copy(fin[:, :, ds(PB * m, PB), 1:2], hs[:, :, :, NB:NB + 1]))
                v.tensor_copy(hs[:, :, :, NBP:NBP + 1], init[:, :, ds(PB * m, PB)].unsqueeze(3)).then_inc(h_ready, 1)

            def y_out(m):
                dve.wait_ge(y_ps, m + 1)
                for j in range(PB):
                    r = slice(32 * j, 32 * j + 32)
                    zu = z[r, ds(m, 1), :].rearrange("p o (c s) -> p (o s) c", s=SB)
                    for s in range(SB):
                        last = v.scalar_tensor_tensor(zu[:, s], zu[:, s], gains[r, ds(8 * G_D + m, 1)],
                                                      sp_[32 * s:32 * s + 32, j // 2, (j % 2) * NB:(j % 2 + 1) * NB],
                                                      ALU.mult, ALU.add)
                last.then_inc(y_evac, 1)

            def ssm_step(m, b, slabs):
                short = len(slabs) == 2
                for j in range(4):
                    if not short:
                        split_l(slabs[j] + AHEAD, j + AHEAD)
                    elif j >= 2:
                        split_l(slabs[j - 2] + AHEAD, slabs[j - 2] + AHEAD)
                    if j == 0:
                        turn_in(m, b)
                    if j == 1:
                        scan_and_turn(m, b)
                    if j == 2:
                        toep_out(m + 1, 1 - b)
                    if j == 3:
                        y_out(m)

            for t in range(8, 12):
                split_l(t + AHEAD, t + AHEAD)
                if t == 10:
                    toep_out(0, 0)
            with dve.Fori(0, 2) as i:
                seq.enter(i, 0, 2 * 7)
                for b in range(2):
                    m = 2 * i + b
                    ssm_step(m, b, [12 + 4 * m + j for j in range(4)])
            seq.leave(2)
            for m in range(4, 7):
                ssm_step(m, m % 2, SSM_SLABS[m])
            turn_in(7, 1)
            scan_and_turn(7, 1)

            dve.wait_ge(dist_ready, 1)
            seq(v.scalar_tensor_tensor(dist[:], dist[:], -1.0, dist[:], ALU.mult, ALU.max))
            for i in range(8):
                for j in range(2):
                    head = 4 * (i // 2) + 2 * j + i % 2
                    r = slice(64 * j, 64 * j + 64)
                    last = v.tensor_scalar(bias[r, i, :], dist[r, :], -2.0 ** (-8.0 * (head + 1) / 16), None, ALU.mult)
            seq(last)
            dve.wait_ge(sink_loaded, 32)

            def score(n, b, c0):
                dve.wait_ge(s_ps, n + 1)
                if not isinstance(n, int) or n >= 2:
                    dve.wait_ge(pt_ps, 2 * n - 2)
                if c0 == 0:
                    last = v.scalar_tensor_tensor(sc[b][:].rearrange("p (r a) c -> p r (a c)", a=2), gp[:, :, 0:384], HD ** -0.5,
                                                  bias[:].rearrange("p (r a) c -> p r (a c)", a=2), ALU.mult, ALU.add)
                else:
                    for par in range(2):
                        last = v.scalar_tensor_tensor(sc[b][:, par::2, c0:192], gp[:, :, 192 * par + c0:192 * par + 192],
                                                      HD ** -0.5, bias[:, par::2, c0:192], ALU.mult, ALU.add)
                last.then_inc(s_read, 1)
                dve.wait_ge(s_read, n + 1)
                seq(v.reduce_max(mstat[:], sc[b][:, :, c0:192], axis=AX.X))
                seq(v.tensor_tensor(mxw[:], mstat[:], sink[:], ALU.max))
                v.tensor_tensor(esink[:, b, :], sink[:], mxw[:], ALU.subtract)
                v.tensor_scalar(negm[:, b, :], mxw[:], -1.0, None, ALU.mult).then_inc(m_ready, 1)

            def band_step(n, b, narrow=True, ahead=True):
                if narrow:
                    for h in range(2):
                        dve.wait_ge(pt_ps, 2 * n + h + 1)
                        v.tensor_copy(ptb[b][:, 4 * h:4 * h + 4, :],
                                      sp_[0:64, 1, :].rearrange("p (i c) -> p i c", i=4)).then_inc(ptb_cp, 1)
                dve.wait_ge(es_ready, n + 1)
                seq(v.tensor_tensor(den[:, b, :], den[:, b, :], esink[:, b, :], ALU.add))
                seq(v.reciprocal(rden[:, b, :], den[:, b, :]))
                if ahead:
                    score(n + 2, b, 0)
                dve.wait_ge(o_ps, n + 1)
                v.tensor_tensor(osb[b][:], sp_[:, 2, :].rearrange("p (i c) -> p i c", i=8),
                                rden[:, b, :].unsqueeze(2).broadcast_to([P, 8, HD]), ALU.mult).then_inc(o_cp, 1)

            score(0, 0, 128)
            y_out(7)
            score(1, 1, 64)
            band_step(0, 0)
            band_step(1, 1, narrow=False)
            with dve.Fori(1, 3) as i:
                seq.enter(i, 1, 8)
                for b in range(2):
                    band_step(2 * i + b, b)
            seq.leave(3)
            band_step(6, 0)
            band_step(7, 1, ahead=False)
            band_step(8, 0, ahead=False)

            dve.wait_ge(state_stored, 16 * 8)
            for k in range(KT):
                cut_l(aL[:, k, :], z[:, 8 + k, :], aH[:, k, :])

            for j in range(8):
                split_l(T_PATT + j + AHEAD, j + AHEAD)
                cut_l(bL[:, j, :], z[:, j, :], bH[:, j, :])
                dve.wait_ge(gsig_ready, j + 1)
                dve.wait_ge(gemm_done, T_PATT + j + 1)
                v.tensor_tensor(halves(m1[:, j, :]), result(j), halves(gsig[:, j % 2]), ALU.mult).then_inc(evac_dve, 1)
            for j in range(8):
                split_l(T_GLU + j + AHEAD, j + AHEAD)
                dve.wait_ge(evac_act, ACT_BEFORE[T_GLU] + j + 1)
                dve.wait_ge(in_l, n_in[0])
                v.tensor_tensor(sq[:, j % 2], raw[:, j % 2], z[:, j, :], ALU.mult).then_inc(raw_ready, 1)
                cut_l(aL[:, j, :], sq[:, j % 2], aH[:, j, :])
            for j in range(8):
                split_l(T_PSSM + j + AHEAD, j + AHEAD)
                dve.wait_ge(gsig_ready, 8 + j + 1)
                dve.wait_ge(gemm_done, T_PSSM + j + 1)
                v.tensor_tensor(halves(sq[:, j % 2]), result(j), halves(gsig[:, j % 2]), ALU.mult).then_inc(evac_dve, 1)
                dve.wait_ge(evac_dve, 8 + j + 1)
                dve.wait_ge(in_l, n_in[0])
                v.tensor_tensor(raw[:, j % 2], sq[:, j % 2], m1[:, j, :], ALU.add).then_inc(raw_ready, 1)
                cut_l(bL[:, j, :], raw[:, j % 2], bH[:, j, :])

            def mem_scale(i):
                dve.wait_ge(mn_ready, i + 1)
                seq(v.reciprocal(memss[:, 4 + i:5 + i], memss[:, 2 + i:3 + i]))
                v.tensor_scalar(memn[:], memr[:], memss[:, 4 + i:5 + i], None, ALU.mult).then_inc(memr_used, 1)

            def mem_cut(i):
                dve.wait_ge(mmh_done, i + 1)
                for k in range(KT):
                    c = slice(i * P, (i + 1) * P)
                    last = v.scalar_tensor_tensor(mmL[:, k, c], sp_[:, 2 + k // 4, (k % 4) * P:(k % 4 + 1) * P],
                                                  gains[:, 8 * G_MEM + k:8 * G_MEM + k + 1], mmH[:, k, c],
                                                  ALU.mult, ALU.subtract)
                last.then_inc(mml_done, 1)

            for j in range(8):
                split_l(T_WOUT + j + AHEAD, j + AHEAD)
                if j in (2, 5):
                    mem_scale(j // 3)
                if j in (4, 7):
                    mem_cut((j - 4) // 3)

            def kv_out(i):
                dve.wait_ge(kvt_ps, i + 1)
                dst = mk if i < 8 else mv
                v.tensor_copy(dst[:, :, (i % 8) * P:(i % 8 + 1) * P],
                              sp_[:, 2 + i % 2, 0:2 * P].rearrange("p (m c) -> p m c", m=2)).then_inc(kvt_cp, 1)

            split_l(T_XK + 3, 3)

            def beside_post(k):
                split_l(T_XK + k + 1 + AHEAD, k + 1 + AHEAD)
                if k:
                    kv_out(k - 1)

            def beside_pre(k):
                if k < 7:
                    split_l(T_XK + k + 9 + AHEAD, k + 9 + AHEAD)
                    kv_out(k + 8)
                    if k == 6:
                        kv_out(15)

            post_norm(1, G_MIX_POST, beside_post)
            kv_out(7)
            pre_norm(2, G_X_PRE, beside_pre)
            for j in range(8):
                split_l(T_XQ + j + AHEAD, j + AHEAD)

            def cross_max(i):
                n = tok[i][1]
                dve.wait_ge(xs_ps, i + 1)
                if i:
                    dve.wait_ge(xm_ready, i)
                if i >= 2:
                    dve.wait_ge(xp_ready, i - 1)
                ps = gp[0:n, 2 * (i % 2):2 * (i % 2) + 2, :].rearrange("p b (h c) -> p b h c", h=2)
                seq(v.reduce_max(mxw[0:n, 0:4].rearrange("p (b h) -> p b h", b=2), ps, axis=AX.X))
                v.tensor_scalar(negm[0:n, i % 2, 0:4], mxw[0:n, 0:4], -1.0 / 16, None, ALU.mult).then_inc(xm_ready, 1)

            def cross_norm(i):
                n = tok[i][1]
                dve.wait_ge(xp_ready, i + 1)
                seq(v.reciprocal(rden[0:n, i % 2, 0:4], den[0:n, i % 2, 0:4]))
                p = pc[i % 2][0:n]
                v.tensor_tensor(p, p, rden[0:n, i % 2, 0:4].unsqueeze(2).broadcast_to([n, 4, NMEM]), ALU.mult) \
                 .then_inc(xn_ready, 1)

            cross_max(0)
            cross_max(1)
            cross_norm(0)
            for i in range(5):
                if i < 4:
                    cross_norm(i + 1)
                if i < 3:
                    cross_max(i + 2)
                t0, n = tok[i]
                dve.wait_ge(ca_h, i + 1)
                c = slice(t0, t0 + n)
                v.tensor_tensor(aL[:, :, c].rearrange("p (b k) q -> p b k q", b=2),
                                sp_[:, 2:4, :].rearrange("p b (k q) -> p b k q", k=4)[:, :, :, 0:n],
                                aH[:, :, c].rearrange("p (b k) q -> p b k q", b=2), ALU.subtract).then_inc(ca_l, 1)
            for j in range(8):
                split_l(T_XO + j + AHEAD, j + AHEAD)
                dve.wait_ge(gemm_done, T_XO + j + 1)
                v.tensor_copy(halves(o[:, j, :]), result(j)).then_inc(evac_dve, 1)
            dve.wait_ge(evac_dve, DVE_BEFORE[T_FF])
            post_norm(3, G_X_POST)
            pre_norm(4, G_FF_PRE)
            seq(v.memset(o[:], 0.0))

            def ff(q, last_one):
                for j in range(8):
                    t = T_FF + 16 * q + j
                    split_l(t + AHEAD, j + AHEAD)
                    dve.wait_ge(evac_act, ACT_BEFORE[T_FF] + 8 * q + j + 1)
                    dve.wait_ge(in_l, n_in[0] + 8 * q + j)
                    v.tensor_tensor(sq[:, j % 2], raw[:, j % 2], raw[:, j % 2], ALU.mult).then_inc(raw_ready, 1)
                    dve.wait_ge(in_h, n_in[0] + 8 * q + j + 1)
                    v.tensor_tensor(bL[:, j, :], sq[:, j % 2], bH[:, j, :], ALU.subtract).then_inc(in_l, 1)
                for j in range(8):
                    t = T_FF + 8 + 16 * q + j
                    if not last_one or j + AHEAD < 8:
                        split_l(t + AHEAD, j + AHEAD)
                    dve.wait_ge(gemm_done, t + 1)
                    v.tensor_tensor(halves(o[:, j, :]), halves(o[:, j, :]), result(j), ALU.add).then_inc(evac_dve, 1)

            with dve.Fori(0, QUARTERS - 1) as q:
                ff(q, False)
            ff(QUARTERS - 1, True)
            dve.wait_ge(evac_dve, DVE_BEFORE[T_FF] + 8 * QUARTERS)
            post_norm(5, G_FF_POST)

        @block.tensor
        def _(pe):
            mm = nc.tensor.matmul
            tr = nc.tensor.transpose

            def gemm(t, j, xh, xl, free, ready=None, cols=((0, HT), (HT, HT))):
                pe.wait_ge(wl_done, t + 1)
                if free is not None:
                    pe.wait_ge(*free)
                s, b = j % 4, 2 * (j % 2)
                for k in range(KT):
                    if ready is not None:
                        pe.wait_ge(in_l, ready + k + 1)
                    for w, y in ((wH[s], xh), (wH[s], xl), (wL[s], xh)):
                        for h, (c0, n) in enumerate(cols):
                            last = mm(gp[:, b + h, 0:n], w[:, k, :], y[:, k, c0:c0 + n],
                                      start=(k == 0 and w is wH[s] and y is xh),
                                      stop=(k == KT - 1 and w is wL[s]))
                last.then_inc(gemm_done, 1)

            pe.wait_ge(const_ready, 1)
            pe.wait_ge(vecs_loaded, 128)
            tr(sp_[:, 3, 0:64], vecs[:], ident[0:64, 0:64]).then_inc(g_ps, 1)
            for i, (t0, n) in enumerate(tok):
                pe.wait_ge(xnt_ready, i + 1)
                if i == 1:
                    pe.wait_ge(g_cp, 1)
                if i >= 2:
                    pe.wait_ge(xl_done, i - 1)
                for k in range(KT):
                    last = tr(sp_[:, (2 * i + k // 4) % 4, (k % 4) * P:(k % 4) * P + n], xn[0:n, i % 2, k * P:(k + 1) * P],
                              ident[0:n, 0:n])
                last.then_inc(xnt_ps, 1)

            n_sq = [0]

            def stats(k):
                n_sq[0] += 1
                pe.wait_ge(sq_ready, n_sq[0])
                for h in range(2):
                    last = mm(sp_[:, h, 0:HT], ones[:], sq[:, k % 2, h * HT:(h + 1) * HT], start=(k == 0), stop=(k == KT - 1))
                last.then_inc(sq_used, 1)

            def z_slab(t, j, ready=None):
                free = None if isinstance(t, int) and t < 2 else (evac_act, t - 1)
                gemm(t, j, aH, aL, free, ready)

            for t in range(8):
                z_slab(t, t, IN_X0 if t == 0 else None)
                if t == 0:
                    pe.wait_ge(st5_loaded, 80)
                    pe.wait_ge(dt_ready, 1)
                    for i in range(5):
                        last = tr(sp_[:, 3, i * PAIRS:(i + 1) * PAIRS], st5[:, i, :], ident[0:PAIRS, 0:PAIRS])
                    last.then_inc(st_ps, 1)
                if t == 1:
                    pe.wait_ge(c_loaded, 32)
                    pe.wait_ge(st_cp, 1)
                    for c in range(2):
                        for i in range(8):
                            last = tr(sp_[0:64, 2 * c + i // 4, (i % 4) * P:(i % 4 + 1) * P], craw[:, c, i, :], ident[:])
                    last.then_inc(st_ps, 1)
                if t == 2:
                    pe.wait_ge(b_loaded, 32)
                    pe.wait_ge(st_cp, 2)
                    for c in range(2):
                        for k in range(16):
                            last = tr(sp_[:, c, k * PAIRS:(k + 1) * PAIRS], braw[:, c, :, k], ident[0:PAIRS, 0:PAIRS])
                    last.then_inc(st_ps, 1)
                for i in {3: (0, 1), 4: (2, 3), 5: (4,)}.get(t, ()):
                    n = tok[i][1]
                    if i == 0:
                        pe.wait_ge(st_cp, 3)
                    for kh in range(2):
                        if i >= 2:
                            pe.wait_ge(xt_cp, 2 * i + kh - 3)
                        for k in range(4):
                            c = (4 * kh + k) * P
                            last = tr(sp_[:, (2 * i + kh) % 4, k * P:k * P + n], xin[0:n, i, c:c + P], ident[0:n, 0:n])
                        last.then_inc(xt_ps, 1)

            def table(m, b, first=False):
                pe.wait_ge(tab_ready, m + 1)
                if first:
                    pe.wait_ge(xt_cp, 10)
                else:
                    pe.wait_ge(v_read, m)
                for c in range(2):
                    for j in range(PB):
                        tr(sp_[:, c, j * P:(j + 1) * P], xm[:, c, j].rearrange("p s k -> p (s k)"), ident[:])
                for j in range(PB):
                    for c in range(2):
                        last = mm(sp_[0:32, 2, j * P:(j + 1) * P], xm[:, c, j, SB - 1, :],
                                  zm[b][:, c, j, 0:SB, :].rearrange("p s k -> p (s k)"), start=(c == 0), stop=(c == 1))
                last.then_inc(tab_ps, 1)

            def inputs(m, b):
                pe.wait_ge(xtab_cp, m + 1)
                pe.wait_ge(toep_cp, m + 1)
                pe.wait_ge(u_built, m + 1)
                for c in (1, 0):
                    if c == 0:
                        pe.wait_ge(y_evac, m + 1)
                    for j in range(PB):
                        last = mm(sp_[:, 2 * c + j // 2, (j % 2) * NB:(j % 2 + 1) * NB], xt[:, c, j, :], ub[b][:, j, :],
                                  start=True, stop=True)
                last.then_inc(v_ps, 1)

            def outputs(m, b, last_one=False):
                pe.wait_ge(h_ready, m + 1)
                if not last_one:
                    pe.wait_ge(xtab_cp, m + 2)
                for j in range(PB):
                    dst = sp_[:, j // 2, (j % 2) * NB:(j % 2 + 1) * NB]
                    for c in range(2):
                        mm(dst, zm[b][:, c, j, 1:SB + 1, :].rearrange("p s k -> p (s k)"), hs[:, c, j, 0:NB],
                           start=(c == 0), stop=False)
                    last = mm(dst, toep[b][:, j, :], ub[b][:, j, :], start=False, stop=True)
                last.then_inc(y_ps, 1)

            z_slab(8, 0)
            z_slab(9, 1)
            table(0, 0, first=True)
            z_slab(10, 2)
            z_slab(11, 3)
            inputs(0, 0)
            def band_scores(n, b, c0, keys):
                pe.wait_ge(qc_ready, n + 1)
                if not isinstance(n, int) or n >= 1:
                    pe.wait_ge(s_read, n)
                for i in range(8):
                    last = mm(gp[:, i // 2, (i % 2) * 192 + c0:(i % 2) * 192 + 192],
                              qc[b][:, i].rearrange("p j q -> p (j q)"), keys(i // 4), start=True, stop=True)
                last.then_inc(s_ps, 1)

            def k_keys(n, c0):
                return lambda h: z[:, 16 + h, ds(CH * n - 2 * CH + c0, 192 - c0)]

            def ssm_step(m, b, slabs):
                half = len(slabs) // 2
                j0 = slabs[0] if isinstance(slabs[0], int) else 0
                for j in range(half):
                    z_slab(slabs[j], j0 + j)
                table(m + 1, 1 - b)
                z_slab(slabs[half], j0 + half)
                outputs(m, b)
                if half == 2:
                    z_slab(slabs[3], 3)
                inputs(m + 1, 1 - b)

            with pe.Fori(0, 2) as i:
                for b in range(2):
                    m = 2 * i + b
                    ssm_step(m, b, [12 + 4 * m + j for j in range(4)])
            for m in range(4, 7):
                ssm_step(m, m % 2, SSM_SLABS[m])

            pe.wait_ge(evac_act, T_PATT)
            for i in range(9):
                if i % 2 == 0 and i >= 8:
                    pe.wait_ge(va_cp, i // 2 - 3)
                n = P if i < 8 else TS
                for h in range(2):
                    last = tr(gp[0:n, (i // 2) % 4, (i % 2) * KV + h * P:(i % 2) * KV + (h + 1) * P],
                              z[:, 18 + h, CH * i:CH * i + n], ident[:])
                if i % 2 or i == 8:
                    last.then_inc(va_ps, 1)
            pe.wait_ge(cache_loaded, 32)
            pe.wait_ge(va_cp, 3)
            for h in range(2):
                tr(gp[:, 1, h * P:(h + 1) * P], z[:, 16 + h, TP - P:TP], ident[:])
                tr(gp[0:TS, 1, KV + h * P:KV + (h + 1) * P], z[:, 16 + h, TP:TT], ident[:])
                last = tr(gp[:, 2, h * P:(h + 1) * P], ck[:, h * P:(h + 1) * P], ident[:])
            last.then_inc(va_ps, 1)
            pe.wait_ge(va_cp, 6)
            band_scores(0, 0, 128, k_keys(0, 128))
            outputs(7, 1, last_one=True)
            for w in range(2):
                for c in range(2):
                    last = tr(sp_[0:PAIRS, 3, (2 * w + c) * P:(2 * w + c + 1) * P], fin[:, c, :, w], ident[:])
            last.then_inc(va_ps, 1)

            def turn_out(n, b):
                pe.wait_ge(o_cp, n + 1)
                if not isinstance(n, int) or n >= 1:
                    pe.wait_ge(att_done, n)
                else:
                    pe.wait_ge(va_cp, 7)
                for r in range(4):
                    last = tr(sp_[:, 3, r * P:(r + 1) * P], osb[b][:, 2 * r:2 * r + 2, :].rearrange("p a c -> p (a c)"), ident[:])
                last.then_inc(ot_ps, 1)

            def band_step(n, b, wide, narrow, v_wide, v_narrow, scores):
                pe.wait_ge(p_ready, n + 1)
                for h in range(2):
                    if not (isinstance(n, int) and n == 0):
                        if wide:
                            if not (isinstance(n, int) and n == 1 and h == 0):
                                pe.wait_ge(pta_cp, 2 * n - 2 + h)
                        if narrow:
                            pe.wait_ge(ptb_cp, 2 * n - 2 + h)
                    elif h:
                        pe.wait_ge(ptb_cp, 1)
                    for i in range(4 * h, 4 * h + 4):
                        c = slice((i % 4) * P, (i % 4 + 1) * P)
                        if wide:
                            w0 = 0 if narrow else 64
                            last = tr(sp_[:, 0, c], sc[b][:, i, w0:w0 + P], ident[:])
                        if narrow:
                            last = tr(sp_[0:64, 1, c], sc[b][:, i, P:192], ident[:])
                    last.then_inc(pt_ps, 1)
                    if h == 0 and not (isinstance(n, int) and n == 0):
                        turn_out(n - 1, 1 - b)
                if scores:
                    scores()
                if wide:
                    pe.wait_ge(pta_cp, 2 * n)
                if narrow:
                    pe.wait_ge(ptb_cp, 2 if isinstance(n, int) and n == 0 else 2 * n)
                for i in range(8):
                    dst = sp_[:, 2, i * HD:(i + 1) * HD]
                    c = slice((i // 2) * HD, (i // 2 + 1) * HD)
                    if wide:
                        last = mm(dst, pta[b][:, i, :], v_wide(c), start=True, stop=not narrow)
                    if narrow:
                        last = mm(dst, ptb[b][:, i, :], v_narrow(c), start=not wide, stop=True)
                last.then_inc(o_ps, 1)

            def v_pair(n):
                return lambda c: vp[:, ds(n, 1), c].rearrange("p o c -> p (o c)")

            def v_one(n):
                return lambda c: vp[0:64, ds(n, 1), c].rearrange("p o c -> p (o c)")

            band_scores(1, 1, 64, k_keys(1, 64))
            pe.wait_ge(y_evac, 9)
            band_step(0, 0, False, True, None, v_one(0), lambda: band_scores(2, 0, 0, k_keys(2, 0)))
            band_step(1, 1, True, False, v_pair(0), None, lambda: band_scores(3, 1, 0, k_keys(3, 0)))
            with pe.Fori(1, 3) as i:
                for b in range(2):
                    n = 2 * i + b
                    band_step(n, b, True, True, v_pair(n - 2), v_one(n), lambda: band_scores(n + 2, b, 0, k_keys(n + 2, 0)))
            band_step(6, 0, True, True, v_pair(4), v_one(6), lambda: band_scores(8, 0, 0, lambda h: ks[:, h, :]))
            band_step(7, 1, True, True, v_pair(5), v_one(7), None)
            band_step(8, 0, True, True, lambda c: cv[:, c], v_one(8), None)
            turn_out(8, 0)

            for j in range(8):
                free = (s_read, 9) if j < 2 else (evac_dve, j - 1)
                gemm(T_PATT + j, j, aH, aL, free, IN_ATT if j == 0 else None)
            for j in range(8):
                free = (evac_dve, 8 + j - 1) if j < 2 else (evac_act, ACT_BEFORE[T_GLU] + j - 1)
                gemm(T_GLU + j, j, bH, bL, free, IN_Y if j == 0 else None)
            for j in range(8):
                free = (evac_act, ACT_BEFORE[T_PSSM] + j - 1) if j < 2 else (evac_dve, 8 + j - 1)
                gemm(T_PSSM + j, j, aH, aL, free, IN_Y2 if j == 0 else None)

            def mem_turn(i):
                pe.wait_ge(memr_used, i + 1)
                if i:
                    pe.wait_ge(mml_done, i)
                for k in range(KT):
                    last = tr(sp_[:, 2 + k // 4, (k % 4) * P:(k % 4 + 1) * P], memn[:, k * P:(k + 1) * P], ident[:])
                last.then_inc(mm_ps, 1)

            for j in range(8):
                free = (evac_dve, 16 + j - 1) if j < 2 else (evac_act, ACT_BEFORE[T_WOUT] + j - 1)
                gemm(T_WOUT + j, j, bH, bL, free, IN_MIX if j == 0 else None)
                if j:
                    stats(j - 1)
                if j in (3, 6):
                    mem_turn(j // 3 - 1)
            stats(7)

            def kv_turn(i):
                pe.wait_ge(evac_act, ACT_BEFORE[T_XK] + i + 1)
                if i >= 2:
                    pe.wait_ge(kvt_cp, i - 1)
                src = mkT[:, i, :] if i < 8 else mvT[:, i % 2, :]
                for m in range(2):
                    last = tr(sp_[:, 2 + i % 2, m * P:(m + 1) * P], src[:, m * P:(m + 1) * P], ident[:])
                last.then_inc(kvt_ps, 1)

            pe.wait_ge(mml_done, 2)
            for j in range(16):
                gemm(T_XK + j, j, mmH, mmL, (evac_act, ACT_BEFORE[T_XK] + j - 1), None, ((0, NMEM),))
                if j:
                    kv_turn(j - 1)
                if 1 <= j <= KT:
                    stats(j - 1)
            kv_turn(15)
            pe.wait_ge(smk_loaded, 16)
            for i in range(4):
                if i < 2:
                    pe.wait_ge(kvt_cp, 15 + i)
                else:
                    pe.wait_ge(smk_cp, i - 1)
                for k in range(2):
                    for m in range(2):
                        c = (2 * i + k) * P
                        last = tr(sp_[:, 2 + i % 2, (2 * k + m) * P:(2 * k + m + 1) * P], smk[:, m, c:c + P], ident[:])
                last.then_inc(smk_ps, 1)
            for j in range(8):
                gemm(T_XQ + j, j, aH, aL, (evac_act, ACT_BEFORE[T_XQ] + j - 1), IN_X1 if j == 0 else None)

            def cross_scores(i):
                t0, n = tok[i]
                keys = mkT if i < 4 else smkT
                if i < 2:
                    pe.wait_ge(evac_act, ACT_BEFORE[T_XO])
                else:
                    pe.wait_ge(xp_ready, i - 1)
                for h in range(4):
                    for d in range(2):
                        last = mm(gp[0:n, 2 * (i % 2) + h // 2, (h % 2) * NMEM:(h % 2 + 1) * NMEM],
                                  xq[:, 2 * h + d, t0:t0 + n], keys[:, 2 * h + d, :], start=(d == 0), stop=(d == 1))
                last.then_inc(xs_ps, 1)

            def cross_mix(i):
                n = tok[i][1]
                vals = mv if i < 4 else smv
                pe.wait_ge(xn_ready, i + 1)
                for half in range(2):
                    if i:
                        pe.wait_ge(xpt_cp, 2 * i - 1 + half)
                    for h in range(2):
                        for m in range(2):
                            last = tr(sp_[:, half, (2 * h + m) * P:(2 * h + m) * P + n],
                                      pc[i % 2][0:n, 2 * half + h, m * P:(m + 1) * P], ident[0:n, 0:n])
                    last.then_inc(xpt_ps, 1)
                if i < 3:
                    cross_scores(i + 2)
                pe.wait_ge(xpt_cp, 2 * i + 2)
                if i:
                    pe.wait_ge(ca_l, i)
                for k in range(KT):
                    for m in range(2):
                        last = mm(sp_[:, 2 + k // 4, (k % 4) * P:(k % 4) * P + n], vals[:, m, k * P:(k + 1) * P],
                                  ptc[:, k // 2, m, 0:n], start=(m == 0), stop=(m == 1))
                last.then_inc(xo_ps, 1)

            pe.wait_ge(smk_cp, 4)
            pe.wait_ge(smv_loaded, 16)
            cross_scores(0)
            cross_scores(1)
            for i in range(5):
                cross_mix(i)

            pe.wait_ge(ca_l, 5)
            pe.wait_ge(xp_ready, 5)
            for j in range(8):
                free = None if j < 2 else (evac_dve, DVE_BEFORE[T_XO] + j - 1)
                gemm(T_XO + j, j, aH, aL, free)
                if j:
                    stats(j - 1)
            stats(7)
            for k in range(KT):
                stats(k)

            def ff(q, last_one):
                for j in range(8):
                    free = (evac_dve, DVE_BEFORE[T_FF] + 8 * q + j - 1) if j < 2 else (evac_act, ACT_BEFORE[T_FF] + 8 * q + j - 1)
                    gemm(T_FF + 16 * q + j, j, aH, aL, free, IN_FF - 8 if j == 0 else None)
                for j in range(8):
                    free = (evac_act, ACT_BEFORE[T_FF] + 8 * q + 8 + j - 1) if j < 2 else (evac_dve, DVE_BEFORE[T_FF] + 8 * q + j - 1)
                    gemm(T_FF + 8 + 16 * q + j, j, bH, bL, free, IN_FF + 8 * q if j == 0 else None)
                    if last_one and j:
                        stats(j - 1)

            with pe.Fori(0, QUARTERS - 1) as q:
                ff(q, False)
            ff(QUARTERS - 1, True)
            stats(7)
            pe.wait_ge(root_ready, 5)
            for k in range(KT):
                pe.wait_ge(x_done, 16 + k + 1)
                if k >= 2:
                    pe.wait_ge(yt_cp, k - 1)
                for i, (t0, n) in enumerate(tok):
                    dst = sp_[0:n, 2 * (k % 2) + i // 4, (i % 4) * P:(i % 4 + 1) * P]
                    last = tr(dst, x[:, k, t0:t0 + n], ident[:])
                last.then_inc(yt_ps, 1)


_INS = ["x_prompt", "x_sample", "mem_prompt", "cache_win_k", "cache_win_v", "state_ssm_re", "state_ssm_im",
        "cache_mem_k", "cache_mem_v", "norm_mix_pre", "norm_mix_post", "w_in", "ssm_a_re", "ssm_a_im", "ssm_log_dt",
        "ssm_b_re", "ssm_b_im", "ssm_c_re", "ssm_c_im", "ssm_d", "w_glu", "attn_sinks", "p_ssm", "p_att", "w_out",
        "norm_x_pre", "norm_x_post", "norm_mem", "w_xq", "w_xk", "w_xv", "w_xo", "norm_ff_pre", "norm_ff_post",
        "w_ff1", "w_ff2"]
_OUTS = [("y_prompt", (1, 512, 1024)), ("y_sample", (1, 64, 1024)), ("win_k_prompt", (1, 1, 128, 4, 64)),
         ("win_v_prompt", (1, 1, 128, 4, 64)), ("ssm_re_prompt", (1, 1, 64, 64)), ("ssm_im_prompt", (1, 1, 64, 64)),
         ("mem_k_prompt", (1, 1, 256, 4, 256)), ("mem_v_prompt", (1, 1, 256, 4, 256)),
         ("win_k_sample", (1, 1, 128, 4, 64)), ("win_v_sample", (1, 1, 128, 4, 64)),
         ("ssm_re_sample", (1, 1, 64, 64)), ("ssm_im_sample", (1, 1, 64, 64))]


def kernel(**inputs):
    import concourse.bacc as bacc
    import numpy as np
    from concourse.bass_utils import run_bass_kernel_spmd

    nc = bacc.Bacc("TRN2", target_bir_lowering=False, num_devices=1)
    arrays, aps = {}, {}
    for name in _INS:
        arr = np.ascontiguousarray(inputs[name])
        arrays[f"in_{name}"] = arr
        aps[name] = nc.dram_tensor(f"in_{name}", arr.shape, mybir.dt.from_np(arr.dtype), kind="ExternalInput").ap()
    for name, shape in _OUTS:
        aps[name] = nc.dram_tensor(f"out_{name}", shape, F32, kind="ExternalOutput").ap()
    build(nc, aps)
    r = run_bass_kernel_spmd(nc, [arrays], core_ids=[0])
    return tuple(r.results[0][f"out_{name}"] for name, _ in _OUTS)
```
